# Optimizing a Trainium2 kernel written in Bass

```python
import jax, jax.numpy as jnp
from jax import lax
import numpy as np

D_MODEL = 1024
BATCH = 1
SEQ = 512
DEPTH = 1

MIX_WIDTH = D_MODEL
N_BRANCH = 3
CONV_A_K = 3
CONF_K = 31
CHUNK = 128
SGU_HEADS = 8
SGU_HEAD_DIM = MIX_WIDTH // SGU_HEADS
D_FF = 4 * D_MODEL
EPS = 1e-6
IN_COLS = 3 * MIX_WIDTH + 2 * MIX_WIDTH + 2 * MIX_WIDTH + N_BRANCH * D_MODEL
SPLITS = tuple(int(s) for s in np.cumsum([MIX_WIDTH] * 7 + [D_MODEL] * 2))

kernel_name = "hybrid_conv_sgu_gated_block"

def rms_norm(x, g):
    xf = x.astype(jnp.float32)
    y = xf * lax.rsqrt(jnp.mean(xf * xf, axis=-1, keepdims=True) + EPS)
    return (y * g.astype(jnp.float32)).astype(x.dtype)

def layer_norm(x, g, b):
    xf = x.astype(jnp.float32)
    mu = jnp.mean(xf, axis=-1, keepdims=True)
    var = jnp.mean(jnp.square(xf - mu), axis=-1, keepdims=True)
    y = (xf - mu) * lax.rsqrt(var + EPS)
    return (y * g.astype(jnp.float32) + b.astype(jnp.float32)).astype(x.dtype)

def causal_dwconv(x, w):
    k, c = w.shape
    return lax.conv_general_dilated(
        x, w[:, None, :].astype(x.dtype), window_strides=(1,), padding=[(k - 1, 0)],
        dimension_numbers=("NWC", "WIO", "NWC"), feature_group_count=c)

def spatial_gating(u, v, ln_g, ln_b, ws, bs):
    b, s, w = v.shape
    v = layer_norm(v, ln_g, ln_b).reshape(b, s // CHUNK, CHUNK, SGU_HEADS, SGU_HEAD_DIM)
    causal = jnp.tril(jnp.ones((CHUNK, CHUNK), dtype=bool))
    ws_c = jnp.where(causal[None], ws, jnp.zeros_like(ws))
    mixed = jnp.einsum("hts,bcshd->bcthd", ws_c, v) + jnp.transpose(bs)[:, :, None]
    return u * mixed.reshape(b, s, w)

def hybrid_mixer(xn, w_in, conv_a_w, conf_dw_w, conf_dw_b, conf_ln_g, conf_ln_b,
                 sgu_ln_g, sgu_ln_b, sgu_ws, sgu_b, w_branch, w_out):
    z = xn @ w_in
    a_h, a_b, a_c, c_a, c_g, s_u, s_v, g_a, g_c, g_s = jnp.split(z, SPLITS, axis=-1)
    y_a = a_b * causal_dwconv(a_c * a_h, conv_a_w)
    y_c = causal_dwconv(c_a * jax.nn.sigmoid(c_g), conf_dw_w) + conf_dw_b
    y_c = jax.nn.silu(layer_norm(y_c, conf_ln_g, conf_ln_b))
    y_s = spatial_gating(jax.nn.gelu(s_u), jax.nn.gelu(s_v), sgu_ln_g, sgu_ln_b, sgu_ws, sgu_b)
    merged = (jax.nn.sigmoid(g_a) * (y_a @ w_branch[0])
              + jax.nn.sigmoid(g_c) * (y_c @ w_branch[1])
              + jax.nn.sigmoid(g_s) * (y_s @ w_branch[2]))
    return merged @ w_out

def setup_inputs(seed: int = 0) -> dict:
    key = jax.random.key(seed)
    ks = jax.random.split(key, 24)
    n = jax.random.normal
    f32 = jnp.float32

    def gain(k, shape):
        return 1.0 + 0.05 * n(k, shape, f32)

    return {
        "x": n(ks[0], (BATCH, SEQ, D_MODEL), f32),
        "norm_mix_pre": gain(ks[1], (DEPTH, D_MODEL)),
        "norm_mix_post": gain(ks[2], (DEPTH, D_MODEL)),
        "norm_ffn_pre": gain(ks[3], (DEPTH, D_MODEL)),
        "norm_ffn_post": gain(ks[4], (DEPTH, D_MODEL)),
        "w_in": n(ks[5], (DEPTH, D_MODEL, IN_COLS), f32) * D_MODEL ** -0.5,
        "conv_a_w": n(ks[6], (DEPTH, CONV_A_K, MIX_WIDTH), f32) * CONV_A_K ** -0.5,
        "conf_dw_w": n(ks[7], (DEPTH, CONF_K, MIX_WIDTH), f32) * CONF_K ** -0.5,
        "conf_dw_b": 0.02 * n(ks[8], (DEPTH, MIX_WIDTH), f32),
        "conf_ln_g": gain(ks[9], (DEPTH, MIX_WIDTH)),
        "conf_ln_b": 0.02 * n(ks[10], (DEPTH, MIX_WIDTH), f32),
        "sgu_ln_g": gain(ks[11], (DEPTH, MIX_WIDTH)),
        "sgu_ln_b": 0.02 * n(ks[12], (DEPTH, MIX_WIDTH), f32),
        "sgu_ws": n(ks[13], (DEPTH, SGU_HEADS, CHUNK, CHUNK), f32) * CHUNK ** -0.5,
        "sgu_b": 1.0 + 0.1 * n(ks[14], (DEPTH, SGU_HEADS, CHUNK), f32),
        "w_branch": n(ks[15], (DEPTH, N_BRANCH, MIX_WIDTH, D_MODEL), f32) * MIX_WIDTH ** -0.5,
        "w_out": n(ks[16], (DEPTH, D_MODEL, D_MODEL), f32) * D_MODEL ** -0.5,
        "w_ff1": n(ks[17], (DEPTH, D_MODEL, D_FF), f32) * D_MODEL ** -0.5,
        "w_ff2": n(ks[18], (DEPTH, D_FF, D_MODEL), f32) * D_FF ** -0.5,
    }

def reference(x, norm_mix_pre, norm_mix_post, norm_ffn_pre, norm_ffn_post, w_in, conv_a_w,
              conf_dw_w, conf_dw_b, conf_ln_g, conf_ln_b, sgu_ln_g, sgu_ln_b, sgu_ws, sgu_b,
              w_branch, w_out, w_ff1, w_ff2):
    for l in range(DEPTH):
        h = rms_norm(x, norm_mix_pre[l])
        m = hybrid_mixer(h, w_in[l], conv_a_w[l], conf_dw_w[l], conf_dw_b[l], conf_ln_g[l],
                         conf_ln_b[l], sgu_ln_g[l], sgu_ln_b[l], sgu_ws[l], sgu_b[l],
                         w_branch[l], w_out[l])
        x = x + rms_norm(m, norm_mix_post[l])
        h = rms_norm(x, norm_ffn_pre[l])
        f = jnp.square(jax.nn.relu(h @ w_ff1[l])) @ w_ff2[l]
        x = x + rms_norm(f, norm_ffn_post[l])
    return x


_drawn_inputs = setup_inputs


def setup_inputs(seed=0):
    import zlib

    import numpy as np

    out = dict(_drawn_inputs(seed))
    spreads = {}
    factors = {'conf_dw_b': 4.471,
     'conf_ln_g': 2.931,
     'conf_ln_b': 8.0,
     'sgu_ln_g': 4.687,
     'sgu_ln_b': 8.0}
    for name, (base, spread) in spreads.items():
        noise = np.random.default_rng([zlib.crc32(name.encode()), seed]).standard_normal(out[name].shape)
        drawn = base * np.exp(spread * noise) if base else spread * noise
        out[name] = __import__('jax').numpy.asarray(drawn.astype(out[name].dtype))
    for name, factor in factors.items():
        out[name] = (out[name] * factor).astype(out[name].dtype)
    return out
```

```python
from contextlib import ExitStack

import concourse.bass as bass
from concourse import mybir

F32 = mybir.dt.float32
F32R = mybir.dt.float32r
ALU = mybir.AluOpType
ACT = mybir.ActivationFunctionType

P = 128
D = 1024
SEQ = 512
KT = D // P
CH = SEQ // P
HALF = D // 2
CONV_A = 3
CONF_K = 31
PAD = CONF_K - 1
QUARTERS = 4
EPS = 1e-6
RING = 4
RAW = 2

COL_A = 0
COL_CONF = COL_A + CONV_A
COL_CONF_B = COL_CONF + CONF_K
COL_LN_G = COL_CONF_B + 1
COL_LN_B = COL_LN_G + 1
COLS = COL_LN_B + 1
ROW_MIX_PRE, ROW_SGU_G, ROW_SGU_B, ROW_MIX_POST, ROW_FFN_PRE, ROW_FFN_POST = range(6)

U_V = 0
U_MIX = U_V + 2 * CH
PER_TILE = 6
U_GATE = U_MIX + PER_TILE * KT
U_OUT = U_GATE + 3 * 2 * KT
U_FF = U_OUT + KT
PER_QUARTER = 2 * KT
UNITS = U_FF + QUARTERS * PER_QUARTER

TAPS_OWN = (4, 4, 3, 4)
TAPS_NEXT = (3, 3)
N_OWN, N_NEXT = sum(TAPS_OWN), sum(TAPS_NEXT)
N_LATE = CONF_K - 1 - N_OWN - N_NEXT


class Count:

    def __init__(self, first, i=None, per=0):
        self.first, self.i, self.per = first, i, per

    def plus(self, n):
        return Count(self.first + n, self.i, self.per)

    def times(self, n, more=0):
        here = n * self.first + more
        return here if self.i is None else self.i * (n * self.per) + here

    @property
    def ring(self):
        return self.first % RING

    @property
    def raw(self):
        return self.first % RAW

    def loads(self):
        here = 16 * (self.first // RAW + 1)
        return here if self.i is None else self.i * (16 * self.per // RAW) + here


def build(nc, x_d, units_d, cols_d, rows_d, ws_d, bs_d, out_d):
    with ExitStack() as ctx:
        def sb(name, shape, dt=F32):
            return ctx.enter_context(nc.sbuf_tensor(name, shape, dt))

        def sem(name):
            return ctx.enter_context(nc.semaphore(name))

        raw = sb("raw", [P, RAW, D])
        w_hi = sb("w_hi", [P, RING, D], F32R)
        w_lo = sb("w_lo", [P, RING, D], F32R)
        a_hi = sb("a_hi", [P, KT, SEQ], F32R)
        a_lo = sb("a_lo", [P, KT, SEQ], F32R)
        b_hi = sb("b_hi", [P, KT, SEQ], F32R)
        b_lo = sb("b_lo", [P, KT, SEQ], F32R)
        c_hi = sb("c_hi", [P, KT, SEQ], F32R)
        c_lo = sb("c_lo", [P, KT, SEQ], F32R)
        wide = sb("wide", [P, CH * D])
        by_token = wide[:, :].rearrange("p (c n) -> p c n", c=CH)
        merged = wide[:, :].rearrange("p (k t) -> p k t", k=KT)
        glu = sb("glu", [P, KT, PAD + SEQ])
        glu_flat = glu[:, :, :].rearrange("p k t -> p (k t)")
        row = [glu_flat[:, n * D:(n + 1) * D] for n in range(3)]
        nrm = glu_flat[:, 0:KT * SEQ].rearrange("p (k t) -> p k t", k=KT)
        conf_flat = sb("conf", [P, KT * SEQ])
        conf = conf_flat[:, :].rearrange("p (k t) -> p k t", k=KT)
        resid = conf_flat[:, :].rearrange("p (c n) -> p c n", c=CH)
        v_hi = sb("v_hi", [P, CH, P], F32R)
        v_lo = sb("v_lo", [P, CH, P], F32R)
        ws_raw = sb("ws_raw", [P, 2, P])
        ws_hi = sb("ws_hi", [P, P], F32R)
        ws_lo = sb("ws_lo", [P, P], F32R)
        bs_row = sb("bs_row", [P, 2, P])
        duo = sb("duo", [P, 2, SEQ])
        th, h_copy = duo[:, 0, :], duo[:, 1, :]
        prod = sb("prod", [P, CONV_A - 1 + SEQ])
        y_a = sb("y_a", [P, SEQ])
        u_act = sb("u_act", [P, SEQ])
        y_s = sb("y_s", [P, SEQ])
        cols = sb("cols", [P, KT, COLS])
        ident = sb("ident", [P, P])
        mean_of = sb("mean_of", [P, P])
        bn = sb("bn", [P, CH, 2, 6])
        mv = sb("mv", [P, CH, 2])
        v_rstd = sb("v_rstd", [P, 2, CH])
        sumsq = sb("sumsq", [P, 4 * CH])
        meansq = sb("meansq", [P, 4 * CH])
        rstd = sb("rstd", [P, 4 * CH])
        power = sb("power", [P, CH])
        ps = ctx.enter_context(nc.psum_tensor("ps", [P, 8, 512], F32))

        raw_loaded = [sem(f"raw_loaded{n}") for n in range(RAW)]
        x_loaded = [sem(f"x_loaded{n}") for n in range(CH)]
        x_again = sem("x_again")
        rows_loaded = sem("rows_loaded")
        rows_again = sem("rows_again")
        cols_loaded = sem("cols_loaded")
        spatial_loaded = [sem(f"spatial_loaded{n}") for n in range(2)]
        w_hi_ready = sem("w_hi_ready")
        w_lo_ready = sem("w_lo_ready")
        unit_done = sem("unit_done")
        consts_ready = sem("consts_ready")
        cols_scaled = sem("cols_scaled")
        sumsq_ready = sem("sumsq_ready")
        meansq_ready = sem("meansq_ready")
        rstd_ready = sem("rstd_ready")
        normed = sem("normed")
        turned = sem("turned")
        act_hi_ready = sem("act_hi_ready")
        act_lo_ready = sem("act_lo_ready")
        v_ready = sem("v_ready")
        bn_ready = sem("bn_ready")
        v_rstd_ready = sem("v_rstd_ready")
        v_normed = sem("v_normed")
        pads_ready = sem("pads_ready")
        th_ready = sem("th_ready")
        glu_ready = sem("glu_ready")
        tap0_ready = sem("tap0_ready")
        conf_tap = sem("conf_tap")
        h_copied = sem("h_copied")
        prod_ready = sem("prod_ready")
        a_tap0 = sem("a_tap0")
        a_step = sem("a_step")
        y_a_hi = sem("y_a_hi")
        y_a_lo = sem("y_a_lo")
        v_hi_ready = sem("v_hi_ready")
        v_lo_ready = sem("v_lo_ready")
        ws_masked = sem("ws_masked")
        ws_hi_ready = sem("ws_hi_ready")
        ws_lo_ready = sem("ws_lo_ready")
        spatial_done = sem("spatial_done")
        u_ready = sem("u_ready")
        s_step = sem("s_step")
        y_s_hi = sem("y_s_hi")
        y_s_lo = sem("y_s_lo")
        gate_ready = sem("gate_ready")
        gated = sem("gated")
        merged_ready = sem("merged_ready")
        merged_hi = sem("merged_hi")
        merged_lo = sem("merged_lo")
        chan_sum = sem("chan_sum")
        stat_done = sem("stat_done")
        centred = sem("centred")
        squared = sem("squared")
        sq_sum = sem("sq_sum")
        var_step = sem("var_step")
        conf_rstd = sem("conf_rstd")
        scaled = sem("scaled")
        affine = sem("affine")
        silu_th = sem("silu_th")
        silu = sem("silu")
        y_c_hi = sem("y_c_hi")
        y_c_lo = sem("y_c_lo")
        chunk_done = sem("chunk_done")
        mixed_in = sem("mixed_in")
        wide_cleared = sem("wide_cleared")
        hidden_relu = sem("hidden_relu")
        hidden_hi = sem("hidden_hi")
        hidden_sq = sem("hidden_sq")
        hidden_lo = sem("hidden_lo")
        mlp_sum = sem("mlp_sum")
        out_step = sem("out_step")
        out_stored = sem("out_stored")

        def chunk_whole(engine, c, before, first_unit):
            if c < CH - 1:
                engine.wait_ge(chunk_done, before + c + 1)
            else:
                engine.wait_ge(unit_done, first_unit + KT)

        block = ctx.enter_context(nc.Block())

        @block.sync
        def _(sp):
            def load(unit, slot):
                sp.dma_start(raw[:, slot, :], units_d[unit]).then_inc(raw_loaded[slot], 16)

            for slot in range(RAW):
                load(slot, slot)
            with sp.Fori(1, UNITS // RAW) as i:
                for slot in range(RAW):
                    sp.wait_ge(w_lo_ready, i * RAW + (slot - RAW + 1))
                    load(i * RAW + slot, slot)
            for c in range(CH):
                sp.wait_ge(out_step, 2 * (c + 1))
                sp.dma_start(out_d[c * P:(c + 1) * P, :], by_token[:, c, :]).then_inc(out_stored, 16)
            sp.wait_ge(out_stored, 16 * CH)

        @block.gpsimd
        def _(pool):
            nc.gpsimd.memset(power[:, :], -0.5).then_inc(consts_ready, 1)
            nc.gpsimd.memset(ident[:, :], 0.0).then_inc(consts_ready, 1)
            nc.gpsimd.memset(mean_of[:, :], 1.0 / D).then_inc(consts_ready, 1)
            pool.wait_ge(consts_ready, 3)
            nc.gpsimd.affine_select(out=ident[:, :], in_=ident[:, :], compare_op=ALU.not_equal,
                                    fill=1.0, base=0, pattern=[[-1, P]],
                                    channel_multiplier=1).then_inc(consts_ready, 1)

            def inverse_rms(n):
                pool.wait_ge(sumsq_ready, n + 1)
                nc.gpsimd.tensor_scalar(meansq[:, n:n + 1], sumsq[:, n:n + 1], 1.0 / D, EPS,
                                        ALU.mult, ALU.add).then_inc(meansq_ready, 1)
                pool.wait_ge(meansq_ready, n + 1)
                nc.gpsimd.tensor_tensor(rstd[:, n:n + 1], meansq[:, n:n + 1], power[:, 0:1],
                                        ALU.pow).then_inc(rstd_ready, 1)

            for c in range(CH):
                inverse_rms(c)

            def load_spatial(j, slot):
                pool.dma_start(ws_raw[:, slot, :], ws_d[j]).then_inc(spatial_loaded[slot], 16)
                pool.dma_start(bs_row[:, slot, :],
                               bs_d[j:j + 1, :].to_broadcast([P, P])).then_inc(spatial_loaded[slot], 16)

            def mask_spatial(slot, loads):
                pool.wait_ge(spatial_loaded[slot], loads)
                nc.gpsimd.affine_select(out=ws_raw[:, slot, :], in_=ws_raw[:, slot, :],
                                        compare_op=ALU.is_ge, fill=0.0, base=0, pattern=[[1, P]],
                                        channel_multiplier=-1).then_inc(ws_masked, 1)

            for j in range(2):
                load_spatial(j, j)
            pool.wait_ge(bn_ready, 3 * CH)
            nc.gpsimd.tensor_scalar(v_rstd[:, 0, :], mv[:, :, 1], 1.0, EPS, ALU.mult,
                                    ALU.add).then_inc(v_rstd_ready, 1)
            pool.wait_ge(v_rstd_ready, 1)
            nc.gpsimd.tensor_tensor(v_rstd[:, 1, :], v_rstd[:, 0, :], power[:, :],
                                    ALU.pow).then_inc(v_rstd_ready, 1)
            for j in range(KT):
                if j >= 2:
                    pool.wait_ge(s_step, 2 * (j - 1))
                    load_spatial(j, j % 2)
                mask_spatial(j % 2, 32 * (j // 2 + 1))

            for j in range(KT):
                pool.wait_ge(conf_tap, KT * (N_OWN + N_NEXT) + N_LATE * (j + 1))
                if j == 0:
                    pool.wait_ge(s_step, 2 * KT)
                    nc.gpsimd.tensor_copy(u_act[:, :], conf[:, j, :]).then_inc(chan_sum, 1)
                else:
                    pool.wait_ge(chan_sum, j)
                    nc.gpsimd.tensor_tensor(u_act[:, :], u_act[:, :], conf[:, j, :],
                                            ALU.add).then_inc(chan_sum, 1)
            for j in range(1, KT):
                pool.wait_ge(squared, j + 1)
                if j > 1:
                    pool.wait_ge(sq_sum, j - 1)
                nc.gpsimd.tensor_tensor(nrm[:, 0, :], nrm[:, 0, :], nrm[:, j, :],
                                        ALU.add).then_inc(sq_sum, 1)

            for n in range(CH, 3 * CH):
                inverse_rms(n)
            pool.wait_ge(turned, 4 * CH)
            nc.gpsimd.memset(wide[:, :], 0.0).then_inc(wide_cleared, 1)
            for n in range(3 * CH, 4 * CH):
                inverse_rms(n)

        @block.scalar
        def _(act):
            def copy_hi(dst, src, scale=1.0):
                return nc.scalar.activation(dst, src, ACT.Copy, scale=scale)

            def split_hi(u, into=None, free=True):
                act.wait_ge(raw_loaded[u.raw], u.loads())
                if free and u.first >= RING:
                    act.wait_ge(unit_done, u.times(1, 1 - RING))
                copy_hi(w_hi[:, u.ring, :] if into is None else into,
                        raw[:, u.raw, :]).then_inc(w_hi_ready, 1)

            def after(u):
                act.wait_ge(unit_done, u.times(1, 1))

            def sum_squares(n, src, dump):
                nc.scalar.activation(dump, src, ACT.Square,
                                     accum_out=sumsq[:, n:n + 1]).then_inc(sumsq_ready, 1)

            def turned_hi(n, c, dst, banks):
                for g in range(2):
                    act.wait_ge(turned, 2 * n + g + 1)
                    copy_hi(dst[:, 4 * g:4 * g + 4, c * P:(c + 1) * P],
                            ps[:, banks + g, :].rearrange("p (k t) -> p k t", k=4)
                            ).then_inc(act_hi_ready, 1)

            for c in range(CH):
                act.dma_start(resid[:, c, :], x_d[c * P:(c + 1) * P, :]).then_inc(x_loaded[c], 16)
                if c == 0:
                    for n, r in enumerate((ROW_MIX_PRE, ROW_SGU_G, ROW_SGU_B)):
                        act.dma_start(row[n], rows_d[r:r + 1, :].to_broadcast([P, D])
                                      ).then_inc(rows_loaded, 16)
            act.dma_start(cols[:, :, :], cols_d).then_inc(cols_loaded, 16)
            for c in range(CH):
                act.wait_ge(x_loaded[c], 16)
                sum_squares(c, resid[:, c, :], by_token[:, c, :])
                if c >= 1:
                    turned_hi(c - 1, c - 1, a_hi, 2 * (c - 1))
                split_hi(Count(c))
            turned_hi(CH - 1, CH - 1, a_hi, 2 * (CH - 1))

            for n in range(2 * CH):
                u = Count(U_V + n)
                after(u)
                if n % CH == CH - 1:
                    half = n // CH
                    for c in range(CH):
                        nc.scalar.activation(by_token[:, c, half * HALF:(half + 1) * HALF],
                                             ps[:, half * CH + c, :],
                                             ACT.Gelu_apprx_tanh).then_inc(v_ready, 1)
                split_hi(u.plus(RING))

            def mix_tile(u, j, b):
                tile = j.times(1)
                after(u)
                if j.first:
                    act.wait_ge(glu_ready, j.times(1))
                nc.scalar.activation(th, ps[:, 0, :], ACT.Tanh, scale=0.5).then_inc(th_ready, 1)
                split_hi(u.plus(RING))
                after(u.plus(1))
                split_hi(u.plus(1 + RING))
                act.wait_ge(cols_scaled, 1)
                act.wait_ge(glu_ready, j.times(1, 1))
                nc.scalar.activation(conf[:, tile, :], glu[:, tile, 0:SEQ], ACT.Identity,
                                     bias=cols[:, tile, COL_CONF_B:COL_CONF_B + 1],
                                     scale=cols[:, tile, COL_CONF:COL_CONF + 1]
                                     ).then_inc(tap0_ready, 1)
                after(u.plus(2))
                if j.first:
                    act.wait_ge(prod_ready, j.times(1))
                nc.scalar.activation(h_copy, ps[:, 2, :], ACT.Copy).then_inc(h_copied, 1)
                split_hi(u.plus(2 + RING))
                after(u.plus(3))
                split_hi(u.plus(3 + RING))
                act.wait_ge(prod_ready, j.times(1, 1))
                if j.first:
                    act.wait_ge(y_a_lo, j.times(1))
                nc.scalar.activation(y_a[:, :], prod[:, 0:SEQ], ACT.Copy,
                                     scale=cols[:, tile, COL_A:COL_A + 1]).then_inc(a_tap0, 1)
                after(u.plus(4))
                split_hi(u.plus(4 + RING))
                if j.first:
                    act.wait_ge(spatial_done, j.times(1))
                act.wait_ge(v_normed, 2 * CH)
                copy_hi(v_hi[:, :, :], by_token[:, :, bass.ds(j.times(P), P)]).then_inc(v_hi_ready, 1)
                act.wait_ge(ws_masked, j.times(1, 1))
                copy_hi(ws_hi[:, :], ws_raw[:, b, :]).then_inc(ws_hi_ready, 1)
                act.wait_ge(a_step, j.times(3, 3))
                copy_hi(b_hi[:, tile, :], y_a[:, :]).then_inc(y_a_hi, 1)
                after(u.plus(5))
                if j.first:
                    act.wait_ge(s_step, j.times(2))
                nc.scalar.activation(u_act[:, :], ps[:, 5, :],
                                     ACT.Gelu_apprx_tanh).then_inc(u_ready, 1)
                split_hi(u.plus(5 + RING))
                act.wait_ge(s_step, j.times(2, 2))
                copy_hi(c_hi[:, tile, :], y_s[:, :]).then_inc(y_s_hi, 1)

            for b in range(2):
                mix_tile(Count(U_MIX + PER_TILE * b), Count(b), b)
            with act.Fori(0, KT // 2 - 1) as i:
                for b in range(2):
                    mix_tile(Count(U_MIX + PER_TILE * (2 + b), i, 2 * PER_TILE), Count(2 + b, i, 2), b)

            def gate(u, n, b):
                after(u)
                if n.first >= 2:
                    act.wait_ge(gated, n.times(1, -1))
                nc.scalar.activation(duo[:, b, :], ps[:, 2 * b, :], ACT.Tanh,
                                     scale=0.5).then_inc(gate_ready, 1)
                split_hi(u.plus(RING))

            def behind_branch(u):
                after(u.plus(1))
                split_hi(u.plus(1 + RING))

            for b in range(2):
                gate(Count(U_GATE + 2 * b), Count(b), b)
                behind_branch(Count(U_GATE + 2 * b))
            with act.Fori(0, KT // 2 - 1) as i:
                for b in range(2):
                    u = Count(U_GATE + 4 + 2 * b, i, 4)
                    gate(u, Count(2 + b, i, 2), b)
                    behind_branch(u)
            for j in range(KT):
                u = Count(U_GATE + 2 * KT + 2 * j)
                gate(u, Count(KT + j), j % 2)
                if j in (1, 2):
                    for t in range(4 * (j - 1), 4 * j):
                        act.wait_ge(centred, t + 1)
                        nc.scalar.activation(nrm[:, t, :], conf[:, t, :], ACT.Square).then_inc(squared, 1)
                if j == 4:
                    act.wait_ge(var_step, 2)
                    nc.scalar.activation(y_s[:, :], y_s[:, :], ACT.Sqrt).then_inc(conf_rstd, 1)
                behind_branch(u)
                for t in SILU_TILES.get(j, ()):
                    act.wait_ge(scaled, t + 1)
                    nc.scalar.activation(nrm[:, t, :], conf[:, t, :], ACT.Identity,
                                         bias=cols[:, t, COL_LN_B:COL_LN_B + 1],
                                         scale=cols[:, t, COL_LN_G:COL_LN_G + 1]).then_inc(affine, 1)
                    act.wait_ge(affine, t + 1)
                    nc.scalar.activation(conf[:, t, :], nrm[:, t, :], ACT.Tanh,
                                         scale=0.5).then_inc(silu_th, 1)
                for t in SILU_TILES.get(j, ()):
                    act.wait_ge(silu, t + 1)
                    copy_hi(b_hi[:, t, :], nrm[:, t, :], 0.5).then_inc(y_c_hi, 1)
            act.wait_ge(y_c_lo, KT)
            act.dma_start(resid[:, :, :], x_d.rearrange("(c p) n -> p c n", p=P)).then_inc(x_again, 16)
            for n, r in enumerate((ROW_MIX_POST, ROW_FFN_PRE, ROW_FFN_POST)):
                act.dma_start(row[n], rows_d[r:r + 1, :].to_broadcast([P, D])).then_inc(rows_again, 16)
            with act.Fori(0, KT // 2) as i:
                for b in range(2):
                    u = Count(U_GATE + 4 * KT + 2 * b, i, 4)
                    j = Count(b, i, 2)
                    gate(u, Count(2 * KT + b, i, 2), b)
                    after(u.plus(1))
                    act.wait_ge(merged_ready, j.times(1, KT + 1))
                    copy_hi(c_hi[:, j.times(1), :], merged[:, j.times(1), :], 0.5).then_inc(merged_hi, 1)
                    split_hi(u.plus(1 + RING))
            for n in range(CH):
                split_hi(Count(U_OUT + CH + n), resident(a_hi, n), free=False)

            for c in range(CH):
                chunk_whole(act, c, 0, U_OUT)
                sum_squares(CH + 2 * c, ps[:, 2 * c:2 * c + 2, :],
                            by_token[:, c, :].rearrange("p (b n) -> p b n", b=2))
                if c:
                    turned_hi(CH + c - 1, c - 1, b_hi, 2 * (c - 1))
                act.wait_ge(mixed_in, 2 * c + 2)
                sum_squares(CH + 2 * c + 1, resid[:, c, :], by_token[:, c, :])
                if c == CH - 2:
                    for n in range(RING):
                        act.wait_ge(unit_done, U_OUT + n + 1)
                        split_hi(Count(U_FF + n), free=False)
            turned_hi(2 * CH - 1, CH - 1, b_hi, 2 * (CH - 1))

            def hidden_unit(u, n):
                after(u)
                if n.first % KT >= 2:
                    act.wait_ge(hidden_lo, n.times(1, -1))
                h = duo[:, n.first % 2, :]
                nc.scalar.activation(h, ps[:, n.first % KT, :], ACT.Relu).then_inc(hidden_relu, 1)
                act.wait_ge(hidden_relu, n.times(1, 1))
                nc.scalar.activation(a_hi[:, n.first % KT, :], h, ACT.Square).then_inc(hidden_hi, 1)
                split_hi(u.plus(RING))

            with act.Fori(0, QUARTERS - 1) as q:
                for n in range(KT):
                    hidden_unit(Count(U_FF + n, q, PER_QUARTER), Count(n, q, KT))
                for n in range(KT):
                    u = Count(U_FF + KT + n, q, PER_QUARTER)
                    after(u)
                    split_hi(u.plus(RING))
            for n in range(KT):
                hidden_unit(Count(U_FF + (QUARTERS - 1) * PER_QUARTER + n), Count((QUARTERS - 1) * KT + n))
            for n in range(CH):
                split_hi(Count(UNITS - CH + n), resident(c_hi, n), free=False)
            for c in range(CH):
                act.wait_ge(mlp_sum, (QUARTERS - 1) * 2 * CH + c + 1)
                sum_squares(3 * CH + c, by_token[:, c, :].rearrange("p (b n) -> p b n", b=2),
                            ps[:, 2 * c:2 * c + 2, :])

        @block.vector
        def _(dve):
            def lo(dst, src, hi, scale=None):
                if scale is None:
                    return nc.vector.tensor_tensor(dst, src, hi, ALU.subtract)
                return nc.vector.scalar_tensor_tensor(out=dst, in0=src, scalar=scale, in1=hi,
                                                      op0=ALU.mult, op1=ALU.subtract)

            def split_lo(u, into=None, hi=None):
                dve.wait_ge(w_hi_ready, u.times(1, 1))
                lo(w_lo[:, u.ring, :] if into is None else into, raw[:, u.raw, :],
                   w_hi[:, u.ring, :] if hi is None else hi).then_inc(w_lo_ready, 1)

            def after(u):
                dve.wait_ge(unit_done, u.times(1, 1))

            def normalise(n, c, src, r, times):
                dve.wait_ge(rstd_ready, n + 1)
                return nc.vector.scalar_tensor_tensor(out=times, in0=src, scalar=rstd[:, n:n + 1],
                                                      in1=r, op0=ALU.mult, op1=ALU.mult)

            def turned_lo(n, c, hi, dst, banks):
                for g in range(2):
                    dve.wait_ge(act_hi_ready, 2 * n + g + 1)
                    lo(dst[:, 4 * g:4 * g + 4, c * P:(c + 1) * P],
                       ps[:, banks + g, :].rearrange("p (k t) -> p k t", k=4),
                       hi[:, 4 * g:4 * g + 4, c * P:(c + 1) * P]).then_inc(act_lo_ready, 1)

            dve.wait_ge(rows_loaded, 48)
            for c in range(CH):
                normalise(c, c, resid[:, c, :], row[0], by_token[:, c, :]).then_inc(normed, 1)
                if c >= 1:
                    turned_lo(c - 1, c - 1, a_hi, a_lo, 2 * (c - 1))
                split_lo(Count(c))
            turned_lo(CH - 1, CH - 1, a_hi, a_lo, 2 * (CH - 1))
            dve.wait_ge(cols_loaded, 16)
            taps = cols[:, :, COL_CONF:COL_CONF + CONF_K]
            nc.vector.tensor_scalar(taps, taps, 0.5, None, ALU.mult).then_inc(cols_scaled, 1)

            def statistics(half):
                for c in range(CH):
                    dve.wait_ge(v_ready, half * CH + c + 1)
                    nc.vector.bn_stats(bn[:, c, half, :],
                                       by_token[:, c, half * HALF:(half + 1) * HALF]).then_inc(bn_ready, 1)

            for n in range(2 * CH):
                u = Count(U_V + n)
                after(u)
                split_lo(u.plus(RING))
                if n == CH:
                    statistics(0)
            statistics(1)
            dve.wait_ge(bn_ready, 2 * CH)
            for c in range(CH):
                nc.vector.bn_aggr(mv[:, c, :], bn[:, c, :, :]).then_inc(bn_ready, 1)
            dve.wait_ge(v_rstd_ready, 2)
            for c in range(CH):
                nc.vector.scalar_tensor_tensor(out=by_token[:, c, :], in0=by_token[:, c, :],
                                               scalar=mv[:, c, 0:1], in1=row[1], op0=ALU.subtract,
                                               op1=ALU.mult).then_inc(v_normed, 1)
            for c in range(CH):
                dve.wait_ge(v_normed, CH + c)
                nc.vector.scalar_tensor_tensor(out=by_token[:, c, :], in0=by_token[:, c, :],
                                               scalar=v_rstd[:, 1, c:c + 1], in1=row[2], op0=ALU.mult,
                                               op1=ALU.add).then_inc(v_normed, 1)
            dve.wait_ge(v_normed, 2 * CH)
            nc.vector.memset(glu[:, :, 0:PAD], 0.0).then_inc(pads_ready, 1)
            nc.vector.memset(prod[:, 0:CONV_A - 1], 0.0).then_inc(pads_ready, 1)
            dve.wait_ge(pads_ready, 2)

            def conf_taps(tile, first, many, before):
                for n in range(many):
                    k = first + n
                    if not (isinstance(before(n), int) and before(n) == 0):
                        dve.wait_ge(conf_tap, before(n))
                    nc.vector.scalar_tensor_tensor(
                        out=conf[:, tile, :], in0=glu[:, tile, k:k + SEQ],
                        scalar=cols[:, tile, COL_CONF + k:COL_CONF + k + 1], in1=conf[:, tile, :],
                        op0=ALU.mult, op1=ALU.add).then_inc(conf_tap, 1)

            def mix_tile(u, j, b, first):
                tile = j.times(1)
                own = 0
                late = 0

                def taps_own(step):
                    nonlocal own
                    done = own
                    own += TAPS_OWN[step]
                    conf_taps(tile, 1 + done, TAPS_OWN[step],
                              lambda n: j.times(N_OWN + N_NEXT, done + n))

                def taps_next(step):
                    nonlocal late
                    if first:
                        return
                    done = late
                    late += TAPS_NEXT[step]
                    conf_taps(j.times(1, -1), 1 + N_OWN + done, TAPS_NEXT[step],
                              lambda n: j.times(N_OWN + N_NEXT, done + n - N_NEXT))

                after(u)
                split_lo(u.plus(RING))
                taps_next(0)
                after(u.plus(1))
                dve.wait_ge(th_ready, j.times(1, 1))
                nc.vector.scalar_tensor_tensor(out=glu[:, tile, PAD:], in0=th, scalar=1.0,
                                               in1=ps[:, 1, :], op0=ALU.add,
                                               op1=ALU.mult).then_inc(glu_ready, 1)
                split_lo(u.plus(1 + RING))
                taps_next(1)
                after(u.plus(2))
                split_lo(u.plus(2 + RING))
                dve.wait_ge(tap0_ready, j.times(1, 1))
                taps_own(0)
                after(u.plus(3))
                dve.wait_ge(h_copied, j.times(1, 1))
                nc.vector.tensor_tensor(prod[:, CONV_A - 1:], ps[:, 3, :], h_copy,
                                        ALU.mult).then_inc(prod_ready, 1)
                split_lo(u.plus(3 + RING))
                taps_own(1)
                dve.wait_ge(a_tap0, j.times(1, 1))
                for k in range(1, CONV_A):
                    if k > 1:
                        dve.wait_ge(a_step, j.times(3, k - 1))
                    nc.vector.scalar_tensor_tensor(
                        out=y_a[:, :], in0=prod[:, k:k + SEQ],
                        scalar=cols[:, tile, COL_A + k:COL_A + k + 1], in1=y_a[:, :],
                        op0=ALU.mult, op1=ALU.add).then_inc(a_step, 1)
                after(u.plus(4))
                dve.wait_ge(a_step, j.times(3, 2))
                nc.vector.tensor_tensor(y_a[:, :], ps[:, 4, :], y_a[:, :], ALU.mult).then_inc(a_step, 1)
                split_lo(u.plus(4 + RING))
                dve.wait_ge(v_hi_ready, j.times(1, 1))
                lo(v_lo[:, :, :], by_token[:, :, bass.ds(j.times(P), P)], v_hi[:, :, :]).then_inc(v_lo_ready, 1)
                dve.wait_ge(ws_hi_ready, j.times(1, 1))
                lo(ws_lo[:, :], ws_raw[:, b, :], ws_hi[:, :]).then_inc(ws_lo_ready, 1)
                taps_own(2)
                dve.wait_ge(y_a_hi, j.times(1, 1))
                lo(b_lo[:, tile, :], y_a[:, :], b_hi[:, tile, :]).then_inc(y_a_lo, 1)
                after(u.plus(5))
                split_lo(u.plus(5 + RING))
                dve.wait_ge(spatial_done, j.times(1, 1))
                by_chunk = "p (c t) -> p c t"
                nc.vector.tensor_tensor(y_s[:, :].rearrange(by_chunk, c=CH),
                                        ps[:, 6, :].rearrange(by_chunk, c=CH),
                                        bs_row[:, b:b + 1, :].to_broadcast([P, CH, P]),
                                        ALU.add).then_inc(s_step, 1)
                dve.wait_ge(u_ready, j.times(1, 1))
                dve.wait_ge(s_step, j.times(2, 1))
                nc.vector.tensor_tensor(y_s[:, :], y_s[:, :], u_act[:, :], ALU.mult).then_inc(s_step, 1)
                taps_own(3)
                dve.wait_ge(y_s_hi, j.times(1, 1))
                lo(c_lo[:, tile, :], y_s[:, :], c_hi[:, tile, :]).then_inc(y_s_lo, 1)

            for b in range(2):
                mix_tile(Count(U_MIX + PER_TILE * b), Count(b), b, first=b == 0)
            with dve.Fori(0, KT // 2 - 1) as i:
                for b in range(2):
                    mix_tile(Count(U_MIX + PER_TILE * (2 + b), i, 2 * PER_TILE), Count(2 + b, i, 2), b,
                             first=False)
            last = KT - 1
            conf_taps(last, 1 + N_OWN, N_NEXT, lambda n: KT * N_OWN + last * N_NEXT + n)

            def add_branch(u, n, j, b, first=False):
                after(u.plus(1))
                dve.wait_ge(gate_ready, n.times(1, 1))
                into = merged[:, j.times(1), :] if first else y_a[:, :]
                if not first and n.first > KT:
                    dve.wait_ge(merged_ready, n.times(1, -KT))
                nc.vector.scalar_tensor_tensor(out=into, in0=duo[:, b, :], scalar=1.0,
                                               in1=ps[:, 2 * b + 1, :], op0=ALU.add,
                                               op1=ALU.mult).then_inc(gated, 1)
                if not first:
                    dve.wait_ge(gated, n.times(1, 1))
                    nc.vector.tensor_tensor(merged[:, j.times(1), :], merged[:, j.times(1), :],
                                            y_a[:, :], ALU.add).then_inc(merged_ready, 1)

            with dve.Fori(0, KT // 2) as i:
                for b in range(2):
                    u = Count(U_GATE + 2 * b, i, 4)
                    j = Count(b, i, 2)
                    after(u)
                    split_lo(u.plus(RING))
                    here = N_LATE // 2
                    base = KT * (N_OWN + N_NEXT)
                    conf_taps(j.times(1), 1 + N_OWN + N_NEXT, here,
                              lambda n: j.times(N_LATE, base + n))
                    add_branch(u, j, j, b, first=True)
                    split_lo(u.plus(1 + RING))
                    conf_taps(j.times(1), 1 + N_OWN + N_NEXT + here, N_LATE - here,
                              lambda n: j.times(N_LATE, base + here + n))
            for j in range(KT):
                u = Count(U_GATE + 2 * KT + 2 * j)
                after(u)
                split_lo(u.plus(RING))
                if j in (1, 2):
                    for t in range(4 * (j - 1), 4 * j):
                        dve.wait_ge(stat_done, 1)
                        nc.vector.tensor_tensor(conf[:, t, :], conf[:, t, :], ps[:, 4, :],
                                                ALU.subtract).then_inc(centred, 1)
                if j == 4:
                    dve.wait_ge(stat_done, 2)
                    nc.vector.tensor_scalar(y_s[:, :], ps[:, 5, :], EPS, None, ALU.add).then_inc(var_step, 1)
                    dve.wait_ge(var_step, 1)
                    nc.vector.reciprocal(y_s[:, :], y_s[:, :]).then_inc(var_step, 1)
                for t in SILU_TILES.get(j, ()):
                    dve.wait_ge(conf_rstd, 1)
                    nc.vector.tensor_tensor(conf[:, t, :], conf[:, t, :], y_s[:, :],
                                            ALU.mult).then_inc(scaled, 1)
                add_branch(u, Count(KT + j), Count(j), j % 2)
                split_lo(u.plus(1 + RING))
                for t in SILU_TILES.get(j, ()):
                    dve.wait_ge(silu_th, t + 1)
                    nc.vector.scalar_tensor_tensor(out=nrm[:, t, :], in0=conf[:, t, :], scalar=1.0,
                                                   in1=nrm[:, t, :], op0=ALU.add,
                                                   op1=ALU.mult).then_inc(silu, 1)
                for t in SILU_TILES.get(j, ()):
                    dve.wait_ge(y_c_hi, t + 1)
                    lo(b_lo[:, t, :], nrm[:, t, :], b_hi[:, t, :], 0.5).then_inc(y_c_lo, 1)
            with dve.Fori(0, KT // 2) as i:
                for b in range(2):
                    u = Count(U_GATE + 4 * KT + 2 * b, i, 4)
                    j = Count(b, i, 2)
                    after(u)
                    split_lo(u.plus(RING))
                    add_branch(u, Count(2 * KT + b, i, 2), j, b)
                    split_lo(u.plus(1 + RING))
                    dve.wait_ge(merged_hi, j.times(1, 1))
                    lo(c_lo[:, j.times(1), :], merged[:, j.times(1), :], c_hi[:, j.times(1), :],
                       0.5).then_inc(merged_lo, 1)
            for n in range(CH):
                split_lo(Count(U_OUT + CH + n), resident(a_lo, n), resident(a_hi, n))

            dve.wait_ge(x_again, 16)
            dve.wait_ge(rows_again, 48)
            for c in range(CH):
                normalise(CH + 2 * c, c, ps[:, 2 * c:2 * c + 2, :],
                          row[0].rearrange("p (b n) -> p b n", b=2),
                          by_token[:, c, :].rearrange("p (b n) -> p b n", b=2)).then_inc(mixed_in, 1)
                dve.wait_ge(mixed_in, 2 * c + 1)
                nc.vector.tensor_tensor(resid[:, c, :], resid[:, c, :], by_token[:, c, :],
                                        ALU.add).then_inc(mixed_in, 1)
                if c:
                    turned_lo(CH + c - 1, c - 1, b_hi, b_lo, 2 * (c - 1))
                normalise(CH + 2 * c + 1, c, resid[:, c, :], row[1],
                          by_token[:, c, :]).then_inc(normed, 1)
                if c == CH - 2:
                    for n in range(RING):
                        split_lo(Count(U_FF + n))
            turned_lo(2 * CH - 1, CH - 1, b_hi, b_lo, 2 * (CH - 1))

            def hidden_unit(u, n):
                place = n.first % KT
                h = duo[:, n.first % 2, :]
                after(u)
                split_lo(u.plus(RING))
                dve.wait_ge(hidden_hi, n.times(1, 1))
                nc.vector.tensor_tensor(h, h, h, ALU.mult).then_inc(hidden_sq, 1)
                dve.wait_ge(hidden_sq, n.times(1, 1))
                lo(a_lo[:, place, :], h, a_hi[:, place, :]).then_inc(hidden_lo, 1)

            dve.wait_ge(wide_cleared, 1)
            with dve.Fori(0, QUARTERS - 1) as q:
                for n in range(KT):
                    hidden_unit(Count(U_FF + n, q, PER_QUARTER), Count(n, q, KT))
                for n in range(KT):
                    u = Count(U_FF + KT + n, q, PER_QUARTER)
                    after(u)
                    if n % CH == CH - 1:
                        half = n // CH
                        for c in range(CH):
                            y = by_token[:, c, half * HALF:(half + 1) * HALF]
                            nc.vector.tensor_tensor(y, y, ps[:, half * CH + c, :],
                                                    ALU.add).then_inc(mlp_sum, 1)
                    split_lo(u.plus(RING))
            for n in range(KT):
                hidden_unit(Count(U_FF + (QUARTERS - 1) * PER_QUARTER + n), Count((QUARTERS - 1) * KT + n))
            for n in range(CH):
                split_lo(Count(UNITS - CH + n), resident(c_lo, n), resident(c_hi, n))

            sums = (QUARTERS - 1) * 2 * CH
            dve.wait_ge(mlp_sum, sums)
            for c in range(CH + 1):
                if c < CH:
                    chunk_whole(dve, c, CH - 1, UNITS - KT)
                    y = by_token[:, c, :].rearrange("p (b n) -> p b n", b=2)
                    nc.vector.tensor_tensor(y, y, ps[:, 2 * c:2 * c + 2, :], ALU.add).then_inc(mlp_sum, 1)
                if c:
                    normalise(3 * CH + c - 1, c - 1, by_token[:, c - 1, :], row[2],
                              by_token[:, c - 1, :]).then_inc(out_step, 1)
                    dve.wait_ge(out_step, 2 * c - 1)
                    nc.vector.tensor_tensor(by_token[:, c - 1, :], by_token[:, c - 1, :],
                                            resid[:, c - 1, :], ALU.add).then_inc(out_step, 1)

        @block.tensor
        def _(pe):
            def products(bank, left_hi, left_lo, right_hi, right_lo, first, final):
                nc.tensor.matmul(ps[:, bank, :], left_hi, right_hi, start=first, stop=False)
                nc.tensor.matmul(ps[:, bank, :], left_hi, right_lo, start=False, stop=False)
                return nc.tensor.matmul(ps[:, bank, :], left_lo, right_hi, start=False, stop=final)

            def ready(u):
                pe.wait_ge(w_lo_ready, u.times(1, 1))

            def channel_unit(u, hi, low, bank, before_tile=None):
                ready(u)
                for k in range(KT):
                    if before_tile:
                        before_tile(k)
                    w = slice(k * P, (k + 1) * P)
                    mm = products(bank, w_hi[:, u.ring, w], w_lo[:, u.ring, w], hi[:, k, :], low[:, k, :],
                                  k == 0, k == KT - 1)
                mm.then_inc(unit_done, 1)

            def token_block(c, piece, hi, low, right_hi, right_lo, bank):
                for n in range(2):
                    k = 2 * piece + n
                    t, w = slice(c * P, (c + 1) * P), slice(n * HALF, (n + 1) * HALF)
                    mm = products(bank, hi[:, k, t], low[:, k, t], right_hi[:, w], right_lo[:, w],
                                  k == 0, k == KT - 1)
                return mm

            def token_unit(u, piece, half, hi, low, before_chunk=None):
                ready(u)
                for c in range(CH):
                    if before_chunk:
                        before_chunk(c)
                    mm = token_block(c, piece, hi, low, w_hi[:, u.ring, :], w_lo[:, u.ring, :],
                                     half * CH + c)
                mm.then_inc(unit_done, 1)

            def turn(n, c, banks):
                pe.wait_ge(normed, n + 1)
                for g in range(2):
                    for k in range(4):
                        at = (4 * g + k) * P
                        mm = nc.tensor.transpose(ps[:, banks + g, k * P:(k + 1) * P],
                                                 by_token[:, c, at:at + P], ident[:, :])
                    mm.then_inc(turned, 1)

            def resident_products(first_unit, hi, low, second_hi, second_lo, chunks_before, between):
                for c in range(CH):
                    for half in range(2):
                        for piece in range(CH):
                            u = Count(first_unit + half * CH + piece)
                            if c == 0:
                                ready(u)
                                between(piece if half == 0 else None)
                            w = ((w_hi[:, u.ring, :], w_lo[:, u.ring, :]) if half == 0 else
                                 (resident(second_hi, piece), resident(second_lo, piece)))
                            mm = token_block(c, piece, hi, low, *w, 2 * c + half)
                            if c == CH - 1:
                                mm.then_inc(unit_done, 1)
                    if c < CH - 1:
                        mm.then_inc(chunk_done, 1)
                    if chunks_before is not None and c:
                        turn(CH + c - 1, c - 1, 2 * (c - 1))

            pe.wait_ge(consts_ready, 4)
            turn(0, 0, 0)

            def first_chunks(c):
                if c + 1 < CH:
                    turn(c + 1, c + 1, 2 * (c + 1))
                pe.wait_ge(act_lo_ready, 2 * (c + 1))

            for n in range(2 * CH):
                token_unit(Count(U_V + n), n % CH, n // CH, a_hi, a_lo, first_chunks if n == 0 else None)

            with pe.Fori(0, KT // 2) as i:
                for b in range(2):
                    j = Count(b, i, 2)
                    for n in range(PER_TILE):
                        channel_unit(Count(U_MIX + PER_TILE * b + n, i, 2 * PER_TILE), a_hi, a_lo, n)
                    pe.wait_ge(v_lo_ready, j.times(1, 1))
                    pe.wait_ge(ws_lo_ready, j.times(1, 1))
                    for c in range(CH):
                        out = ps[:, 6, c * P:(c + 1) * P]
                        nc.tensor.matmul(out, v_hi[:, c, :], ws_hi[:, :], start=True, stop=False)
                        nc.tensor.matmul(out, v_hi[:, c, :], ws_lo[:, :], start=False, stop=False)
                        mm = nc.tensor.matmul(out, v_lo[:, c, :], ws_hi[:, :], start=False, stop=True)
                    mm.then_inc(spatial_done, 1)

            def pair(u, hi, low, b, before_tile=None):
                channel_unit(u, a_hi, a_lo, 2 * b)
                channel_unit(u.plus(1), hi, low, 2 * b + 1, before_tile)

            pe.wait_ge(y_a_lo, KT)
            with pe.Fori(0, KT // 2) as i:
                for b in range(2):
                    pair(Count(U_GATE + 2 * b, i, 4), b_hi, b_lo, b)
            pe.wait_ge(y_s_lo, KT)
            for j in range(KT):
                pair(Count(U_GATE + 2 * KT + 2 * j), c_hi, c_lo, j % 2)
                if j == 0:
                    pe.wait_ge(chan_sum, KT)
                    nc.tensor.matmul(ps[:, 4, :], mean_of[:, :], u_act[:, :], start=True,
                                     stop=True).then_inc(stat_done, 1)
                if j == 3:
                    pe.wait_ge(sq_sum, KT - 1)
                    nc.tensor.matmul(ps[:, 5, :], mean_of[:, :], nrm[:, 0, :], start=True,
                                     stop=True).then_inc(stat_done, 1)
            first_gate = Count(U_GATE + 4 * KT)
            channel_unit(first_gate, a_hi, a_lo, 0)
            channel_unit(first_gate.plus(1), b_hi, b_lo, 1, lambda k: pe.wait_ge(y_c_lo, k + 1))
            pair(first_gate.plus(2), b_hi, b_lo, 1)
            with pe.Fori(0, KT // 2 - 1) as i:
                for b in range(2):
                    pair(Count(U_GATE + 4 * KT + 4 + 2 * b, i, 4), b_hi, b_lo, b)

            resident_products(U_OUT, c_hi, c_lo, a_hi, a_lo, CH,
                              lambda piece: piece is not None and pe.wait_ge(merged_lo, 2 * piece + 2))
            turn(2 * CH - 1, CH - 1, 2 * (CH - 1))

            def up(u, n):
                channel_unit(u, b_hi, b_lo, n)

            pe.wait_ge(act_lo_ready, 4 * CH)
            with pe.Fori(0, QUARTERS - 1) as q:
                for n in range(KT):
                    up(Count(U_FF + n, q, PER_QUARTER), n)
                for n in range(KT):
                    if n < CH:
                        pe.wait_ge(hidden_lo, Count(0, q, KT).times(1, 2 * n + 2))
                    token_unit(Count(U_FF + KT + n, q, PER_QUARTER), n % CH, n // CH, a_hi, a_lo)
            for n in range(KT):
                up(Count(U_FF + (QUARTERS - 1) * PER_QUARTER + n), n)
            before = (QUARTERS - 1) * KT
            resident_products(UNITS - KT, a_hi, a_lo, c_hi, c_lo, None,
                              lambda piece: piece is not None and
                              pe.wait_ge(hidden_lo, before + 2 * piece + 2))


SILU_TILES = {5: (0, 1, 2), 6: (3, 4, 5), 7: (6, 7)}


def resident(buffer, n):
    return buffer[:, 2 * n:2 * n + 2, :].rearrange("p k t -> p (k t)")


def kernel(x, norm_mix_pre, norm_mix_post, norm_ffn_pre, norm_ffn_post, w_in, conv_a_w, conf_dw_w,
           conf_dw_b, conf_ln_g, conf_ln_b, sgu_ln_g, sgu_ln_b, sgu_ws, sgu_b, w_branch, w_out,
           w_ff1, w_ff2):
    import numpy as np
    import concourse.bacc as bacc
    from concourse.bass_utils import run_bass_kernel_spmd

    def channel_units(w):
        return w.reshape(KT, P, -1, P).transpose(2, 1, 0, 3).reshape(-1, P, D)

    def token_units(w):
        return w.reshape(CH, 2, P, 2, HALF).transpose(3, 0, 2, 1, 4).reshape(-1, P, D)

    a_h, a_b, a_c, c_a, c_g, s_u, s_v, g_a, g_c, g_s = np.split(np.asarray(w_in)[0], 10, axis=1)
    w_branch, w_out = np.asarray(w_branch)[0], np.asarray(w_out)[0]
    w_ff1, w_ff2 = np.asarray(w_ff1)[0], np.asarray(w_ff2)[0]

    def interleave(*parts):
        return np.stack([channel_units(p) for p in parts], axis=1).reshape(-1, P, D)

    units = [token_units(s_v), interleave(c_g, c_a, a_h, a_c, a_b, s_u), interleave(g_a, w_branch[0]),
             interleave(g_s, w_branch[2]), interleave(g_c, w_branch[1]), token_units(w_out)]
    for q in range(QUARTERS):
        units += [channel_units(w_ff1[:, q * D:(q + 1) * D]), token_units(w_ff2[q * D:(q + 1) * D])]
    by_channel = np.concatenate([np.asarray(a)[0].reshape(-1, D) for a in
                                 (conv_a_w, conf_dw_w, conf_dw_b, conf_ln_g, conf_ln_b)])
    arrays = {
        "x_in": np.asarray(x)[0],
        "units_in": np.concatenate(units),
        "cols_in": by_channel.reshape(COLS, KT, P).transpose(2, 1, 0),
        "rows_in": np.concatenate([np.asarray(a) for a in (norm_mix_pre, sgu_ln_g, sgu_ln_b,
                                                           norm_mix_post, norm_ffn_pre, norm_ffn_post)]),
        "ws_in": np.asarray(sgu_ws)[0].transpose(0, 2, 1),
        "bs_in": np.asarray(sgu_b)[0],
    }
    arrays = {name: np.ascontiguousarray(a) for name, a in arrays.items()}
    nc = bacc.Bacc("TRN2", target_bir_lowering=False, num_devices=1)
    ins = [nc.dram_tensor(name, a.shape, F32, kind="ExternalInput").ap() for name, a in arrays.items()]
    out = nc.dram_tensor("y_out", (SEQ, D), F32, kind="ExternalOutput").ap()
    build(nc, *ins, out)
    result = run_bass_kernel_spmd(nc, [arrays], core_ids=[0])
    return result.results[0]["y_out"].reshape(1, SEQ, D)
```

```python
from contextlib import ExitStack

import concourse.bass as bass
from concourse import mybir

F32 = mybir.dt.float32
F32R = mybir.dt.float32r
ALU = mybir.AluOpType
ACT = mybir.ActivationFunctionType

P = 128
D = 1024
SEQ = 512
KT = D // P
CH = SEQ // P
HALF = D // 2
CONV_A = 3
CONF_K = 31
PAD = CONF_K - 1
QUARTERS = 4
EPS = 1e-6
ROOT_D = 32
assert ROOT_D ** 2 == D
RING = 4
RAW = 2
EARLY = 3

COL_A = 0
COL_CONF = COL_A + CONV_A
COL_CONF_B = COL_CONF + CONF_K
COL_LN_G = COL_CONF_B + 1
COL_LN_B = COL_LN_G + 1
COL_SGU_G = COL_LN_B + 1
COL_SGU_B = COL_SGU_G + 1
COLS = COL_SGU_B + 1
ROW_MIX_PRE, ROW_MIX_POST, ROW_FFN_PRE, ROW_FFN_POST = range(4)

U_V = 0
U_MIX = U_V + 2 * CH
PER_TILE = 6
U_GATE = U_MIX + PER_TILE * KT
U_OUT = U_GATE + 3 * 2 * KT
U_FF = U_OUT + KT
PER_QUARTER = 2 * KT
UNITS = U_FF + QUARTERS * PER_QUARTER

TAPS_OWN = (4, 4, 3, 4)
TAPS_NEXT = (3, 3)
N_OWN, N_NEXT = sum(TAPS_OWN), sum(TAPS_NEXT)
N_LATE = CONF_K - 1 - N_OWN - N_NEXT


BLOCKS = ((0, 0), (1, 0), (2, 0), (0, 1), (1, 1), (2, 1), (3, 0), (3, 1))
BLOCK_PIECES = ([(n, piece) for n in range(2) for piece in range(CH - 1)] +
                [(n, CH - 1) for n in range(2)] +
                [(n, piece) for n in range(2, len(BLOCKS)) for piece in range(CH)])


class Count:

    def __init__(self, first, i=None, per=0):
        self.first, self.i, self.per = first, i, per

    def plus(self, n):
        return Count(self.first + n, self.i, self.per)

    def times(self, n, more=0):
        here = n * self.first + more
        return here if self.i is None else self.i * (n * self.per) + here

    @property
    def ring(self):
        return self.first % RING

    @property
    def raw(self):
        return self.first % RAW

    def loads(self):
        here = 16 * (self.first // RAW + 1)
        return here if self.i is None else self.i * (16 * self.per // RAW) + here


def build(nc, x_d, units_d, cols_d, rows_d, ws_d, bs_d, out_d):
    with ExitStack() as ctx:
        def sb(name, shape, dt=F32):
            return ctx.enter_context(nc.sbuf_tensor(name, shape, dt))

        def sem(name):
            return ctx.enter_context(nc.semaphore(name))

        raw = sb("raw", [P, RAW, D])
        w_hi = sb("w_hi", [P, RING, D], F32R)
        w_lo = sb("w_lo", [P, RING, D], F32R)
        a_hi = sb("a_hi", [P, KT, SEQ], F32R)
        a_lo = sb("a_lo", [P, KT, SEQ], F32R)
        b_hi = sb("b_hi", [P, KT, SEQ], F32R)
        b_lo = sb("b_lo", [P, KT, SEQ], F32R)
        c_hi = sb("c_hi", [P, KT, SEQ], F32R)
        c_lo = sb("c_lo", [P, KT, SEQ], F32R)
        wide = sb("wide", [P, CH * D])
        by_token = wide[:, :].rearrange("p (c n) -> p c n", c=CH)
        merged = wide[:, :].rearrange("p (k t) -> p k t", k=KT)
        glu = sb("glu", [P, KT, PAD + SEQ])
        glu_flat = glu[:, :, :].rearrange("p k t -> p (k t)")
        row = [glu_flat[:, n * D:(n + 1) * D] for n in range(3)]
        weighted = glu_flat[:, 3 * D:4 * D]
        nrm = glu_flat[:, 0:KT * SEQ].rearrange("p (k t) -> p k t", k=KT)
        conf_flat = sb("conf", [P, KT * SEQ])
        conf = conf_flat[:, :].rearrange("p (k t) -> p k t", k=KT)
        resid = conf_flat[:, :].rearrange("p (c n) -> p c n", c=CH)
        v_hi = sb("v_hi", [P, CH, P], F32R)
        v_lo = sb("v_lo", [P, CH, P], F32R)
        ws_raw = sb("ws_raw", [P, 2, P])
        ws_hi = sb("ws_hi", [P, P], F32R)
        ws_lo = sb("ws_lo", [P, P], F32R)
        bs_row = sb("bs_row", [P, 2, P])
        duo = sb("duo", [P, 2, SEQ])
        th, h_copy = duo[:, 0, :], duo[:, 1, :]
        prod = sb("prod", [P, CONV_A - 1 + SEQ])
        y_a = sb("y_a", [P, SEQ])
        u_act = sb("u_act", [P, SEQ])
        y_s = sb("y_s", [P, SEQ])
        cols = sb("cols", [P, KT, COLS])
        ident = sb("ident", [P, P])
        mean_of = sb("mean_of", [P, P])
        ones = sb("ones", [P, P], F32R)
        bias = sb("bias", [P, P])
        bn = sb("bn", [P, CH, 2, 6])
        mv = sb("mv", [P, CH, 2])
        v_rstd = sb("v_rstd", [P, 2, CH])
        meansq = sb("meansq", [P, 6 * CH])
        meansq_eps = sb("meansq_eps", [P, 4 * CH])
        rstd = sb("rstd", [P, 4 * CH])
        power = sb("power", [P, CH])
        ps = ctx.enter_context(nc.psum_tensor("ps", [P, 8, 512], F32))

        raw_loaded = [sem(f"raw_loaded{n}") for n in range(RAW)]
        x_loaded = [sem(f"x_loaded{n}") for n in range(CH)]
        x_again = sem("x_again")
        rows_loaded = sem("rows_loaded")
        rows_again = sem("rows_again")
        cols_loaded = sem("cols_loaded")
        spatial_loaded = [sem(f"spatial_loaded{n}") for n in range(2)]
        w_hi_ready = sem("w_hi_ready")
        w_lo_ready = sem("w_lo_ready")
        unit_done = sem("unit_done")
        consts_ready = sem("consts_ready")
        cols_scaled = sem("cols_scaled")
        meansq_ready = sem("meansq_ready")
        guarded_meansq = sem("guarded_meansq")
        rstd_ready = sem("rstd_ready")
        normed = sem("normed")
        turned = sem("turned")
        act_hi_ready = sem("act_hi_ready")
        act_lo_ready = sem("act_lo_ready")
        v_ready = sem("v_ready")
        bn_ready = sem("bn_ready")
        v_rstd_ready = sem("v_rstd_ready")
        v_normed = sem("v_normed")
        pads_ready = sem("pads_ready")
        th_ready = sem("th_ready")
        glu_ready = sem("glu_ready")
        tap0_ready = sem("tap0_ready")
        conf_tap = sem("conf_tap")
        h_copied = sem("h_copied")
        prod_ready = sem("prod_ready")
        a_tap0 = sem("a_tap0")
        a_step = sem("a_step")
        y_a_hi = sem("y_a_hi")
        y_a_lo = sem("y_a_lo")
        v_hi_ready = sem("v_hi_ready")
        v_lo_ready = sem("v_lo_ready")
        ws_masked = sem("ws_masked")
        ws_hi_ready = sem("ws_hi_ready")
        ws_lo_ready = sem("ws_lo_ready")
        spatial_done = sem("spatial_done")
        u_ready = sem("u_ready")
        s_step = sem("s_step")
        y_s_hi = sem("y_s_hi")
        y_s_lo = sem("y_s_lo")
        gate_ready = sem("gate_ready")
        gated = sem("gated")
        merged_ready = sem("merged_ready")
        merged_hi = sem("merged_hi")
        merged_lo = sem("merged_lo")
        chan_sum = sem("chan_sum")
        stat_done = sem("stat_done")
        centred = sem("centred")
        squared = sem("squared")
        sq_sum = sem("sq_sum")
        var_step = sem("var_step")
        conf_rstd = sem("conf_rstd")
        scaled = sem("scaled")
        affine = sem("affine")
        silu_th = sem("silu_th")
        silu = sem("silu")
        y_c_hi = sem("y_c_hi")
        y_c_lo = sem("y_c_lo")
        block_done = sem("block_done")
        mixed_in = sem("mixed_in")
        wide_cleared = sem("wide_cleared")
        hidden_relu = sem("hidden_relu")
        hidden_hi = sem("hidden_hi")
        hidden_sq = sem("hidden_sq")
        hidden_lo = sem("hidden_lo")
        mlp_sum = sem("mlp_sum")
        out_weighted = sem("out_weighted")
        out_ready = sem("out_ready")
        out_stored = sem("out_stored")

        def block_whole(engine, c, half, before, first_unit):
            if c < CH - 1:
                engine.wait_ge(block_done, before + BLOCKS.index((c, half)) + 1)
            else:
                engine.wait_ge(unit_done, first_unit + CH * (half + 1))

        block = ctx.enter_context(nc.Block())

        @block.sync
        def _(sp):
            def load(unit, slot):
                sp.dma_start(raw[:, slot, :], units_d[unit]).then_inc(raw_loaded[slot], 16)

            for c in range(CH):
                sp.dma_start(resid[:, c, :], x_d[c * P:(c + 1) * P, :]).then_inc(x_loaded[c], 16)
                if c < RAW:
                    load(c, c)
            sp.dma_start(cols[:, :, :], cols_d).then_inc(cols_loaded, 16)
            with sp.Fori(1, UNITS // RAW) as i:
                for slot in range(RAW):
                    sp.wait_ge(w_lo_ready, i * RAW + (slot - RAW + 1))
                    load(i * RAW + slot, slot)
            for c in range(CH):
                for half in range(2):
                    sp.wait_ge(out_ready, 2 * c + half + 1)
                    w = slice(half * HALF, (half + 1) * HALF)
                    sp.dma_start(out_d[c * P:(c + 1) * P, w], by_token[:, c, w]).then_inc(out_stored, 16)
            sp.wait_ge(out_stored, 16 * 2 * CH)

        @block.gpsimd
        def _(pool):
            nc.gpsimd.memset(power[:, :], -0.5).then_inc(consts_ready, 1)
            nc.gpsimd.memset(ident[:, :], 0.0).then_inc(consts_ready, 1)
            nc.gpsimd.memset(mean_of[:, :], 1.0 / D).then_inc(consts_ready, 1)
            nc.gpsimd.memset(ones[:, :].bitcast(F32), 1.0).then_inc(consts_ready, 1)
            pool.wait_ge(consts_ready, 4)
            nc.gpsimd.affine_select(out=ident[:, :], in_=ident[:, :], compare_op=ALU.not_equal,
                                    fill=1.0, base=0, pattern=[[-1, P]],
                                    channel_multiplier=1).then_inc(consts_ready, 1)

            steps = 0

            def inverse_rms(n, column, halves=False):
                nonlocal steps
                pool.wait_ge(meansq_ready, column + 1 + halves)
                other = meansq[:, column + 1:column + 2] if halves else 0.0
                nc.gpsimd.tensor_scalar(meansq_eps[:, n:n + 1], meansq[:, column:column + 1], other, EPS,
                                        ALU.add, ALU.add).then_inc(guarded_meansq, 1)
                steps += 1
                pool.wait_ge(guarded_meansq, steps)
                nc.gpsimd.tensor_tensor(rstd[:, n:n + 1], meansq_eps[:, n:n + 1], power[:, 0:1],
                                        ALU.pow).then_inc(rstd_ready, 1)

            for c in range(CH):
                inverse_rms(c, c)

            def load_spatial(j, slot):
                pool.dma_start(ws_raw[:, slot, :], ws_d[j]).then_inc(spatial_loaded[slot], 16)
                pool.dma_start(bs_row[:, slot, :],
                               bs_d[j:j + 1, :].to_broadcast([P, P])).then_inc(spatial_loaded[slot], 16)

            def mask_spatial(slot, loads):
                pool.wait_ge(spatial_loaded[slot], loads)
                nc.gpsimd.affine_select(out=ws_raw[:, slot, :], in_=ws_raw[:, slot, :],
                                        compare_op=ALU.is_ge, fill=0.0, base=0, pattern=[[1, P]],
                                        channel_multiplier=-1).then_inc(ws_masked, 1)

            for j in range(2):
                load_spatial(j, j)
            pool.wait_ge(bn_ready, 3 * CH)
            nc.gpsimd.tensor_scalar(v_rstd[:, 0, :], mv[:, :, 1], 1.0, EPS, ALU.mult,
                                    ALU.add).then_inc(v_rstd_ready, 1)
            pool.wait_ge(v_rstd_ready, 1)
            nc.gpsimd.tensor_tensor(v_rstd[:, 1, :], v_rstd[:, 0, :], power[:, :],
                                    ALU.pow).then_inc(v_rstd_ready, 1)
            for j in range(KT):
                if j >= 2:
                    pool.wait_ge(s_step, 3 * (j - 1))
                    load_spatial(j, j % 2)
                mask_spatial(j % 2, 32 * (j // 2 + 1))

            for j in range(KT):
                pool.wait_ge(conf_tap, KT * (N_OWN + N_NEXT) + N_LATE * (j + 1))
                if j == 0:
                    pool.wait_ge(s_step, 3 * KT)
                    nc.gpsimd.tensor_copy(u_act[:, :], conf[:, j, :]).then_inc(chan_sum, 1)
                else:
                    pool.wait_ge(chan_sum, j)
                    nc.gpsimd.tensor_tensor(u_act[:, :], u_act[:, :], conf[:, j, :],
                                            ALU.add).then_inc(chan_sum, 1)
            for j in range(1, KT):
                pool.wait_ge(squared, j + 1)
                if j > 1:
                    pool.wait_ge(sq_sum, j - 1)
                nc.gpsimd.tensor_tensor(nrm[:, 0, :], nrm[:, 0, :], nrm[:, j, :],
                                        ALU.add).then_inc(sq_sum, 1)

            for c in range(CH):
                inverse_rms(CH + 2 * c, CH + 3 * c, halves=True)
                inverse_rms(CH + 2 * c + 1, CH + 3 * c + 2)
            pool.wait_ge(turned, 4 * CH)
            nc.gpsimd.memset(wide[:, :], 0.0).then_inc(wide_cleared, 1)
            for c in range(CH):
                inverse_rms(3 * CH + c, 4 * CH + 2 * c, halves=True)

        @block.scalar
        def _(act):
            def copy_hi(dst, src, scale=1.0):
                return nc.scalar.activation(dst, src, ACT.Copy, scale=scale)

            def split_hi(u, into=None, free=True):
                act.wait_ge(raw_loaded[u.raw], u.loads())
                if free and u.first >= RING:
                    act.wait_ge(unit_done, u.times(1, 1 - RING))
                copy_hi(w_hi[:, u.ring, :] if into is None else into,
                        raw[:, u.raw, :]).then_inc(w_hi_ready, 1)

            def after(u):
                act.wait_ge(unit_done, u.times(1, 1))

            def sum_squares(n, src, dump):
                nc.scalar.activation(dump, src, ACT.Square, scale=1 / ROOT_D,
                                     accum_out=meansq[:, n:n + 1]).then_inc(meansq_ready, 1)

            def turned_hi(n, c, dst, banks):
                for g in range(2):
                    act.wait_ge(turned, 2 * n + g + 1)
                    copy_hi(dst[:, 4 * g:4 * g + 4, c * P:(c + 1) * P],
                            ps[:, banks + g, :].rearrange("p (k t) -> p k t", k=4)
                            ).then_inc(act_hi_ready, 1)

            act.dma_start(row[0], rows_d[ROW_MIX_PRE:ROW_MIX_PRE + 1, :].to_broadcast([P, D])
                          ).then_inc(rows_loaded, 16)
            for c in range(CH):
                act.wait_ge(x_loaded[c], 16)
                sum_squares(c, resid[:, c, :].rearrange("p (b n) -> p b n", b=2),
                            ps[:, 2 * c:2 * c + 2, :])
                if c != 1:
                    split_hi(Count(max(c - 1, 0)))
                if c >= 1:
                    turned_hi(c - 1, c - 1, a_hi, 2 * (c - 1))
            split_hi(Count(CH - 1))
            turned_hi(CH - 1, CH - 1, a_hi, 2 * (CH - 1))

            for n in range(2 * CH):
                u = Count(U_V + n)
                after(u)
                if n % CH == CH - 1:
                    half = n // CH
                    for c in range(CH):
                        nc.scalar.activation(by_token[:, c, half * HALF:(half + 1) * HALF],
                                             ps[:, half * CH + c, :],
                                             ACT.Gelu_apprx_tanh).then_inc(v_ready, 1)
                split_hi(u.plus(RING))

            def mix_tile(u, j, b):
                tile = j.times(1)
                after(u)
                if j.first:
                    act.wait_ge(glu_ready, j.times(1))
                nc.scalar.activation(th, ps[:, 0, :], ACT.Tanh, scale=0.5).then_inc(th_ready, 1)
                split_hi(u.plus(RING))
                after(u.plus(1))
                split_hi(u.plus(1 + RING))
                act.wait_ge(cols_scaled, 1)
                act.wait_ge(glu_ready, j.times(1, 1))
                nc.scalar.activation(conf[:, tile, :], glu[:, tile, 0:SEQ], ACT.Identity,
                                     bias=cols[:, tile, COL_CONF_B:COL_CONF_B + 1],
                                     scale=cols[:, tile, COL_CONF:COL_CONF + 1]
                                     ).then_inc(tap0_ready, 1)
                if j.first:
                    act.wait_ge(spatial_done, j.times(1))
                act.wait_ge(v_normed, CH)
                copy_hi(v_hi[:, :, :], by_token[:, :, bass.ds(j.times(P), P)]).then_inc(v_hi_ready, 1)
                act.wait_ge(ws_masked, j.times(1, 1))
                copy_hi(ws_hi[:, :], ws_raw[:, b, :]).then_inc(ws_hi_ready, 1)
                after(u.plus(2))
                if j.first:
                    act.wait_ge(prod_ready, j.times(1))
                nc.scalar.activation(h_copy, ps[:, 2, :], ACT.Copy).then_inc(h_copied, 1)
                split_hi(u.plus(2 + RING))
                after(u.plus(3))
                split_hi(u.plus(3 + RING))
                act.wait_ge(prod_ready, j.times(1, 1))
                if j.first:
                    act.wait_ge(y_a_lo, j.times(1))
                nc.scalar.activation(y_a[:, :], prod[:, 0:SEQ], ACT.Copy,
                                     scale=cols[:, tile, COL_A:COL_A + 1]).then_inc(a_tap0, 1)
                after(u.plus(4))
                split_hi(u.plus(4 + RING))
                act.wait_ge(a_step, j.times(3, 3))
                copy_hi(b_hi[:, tile, :], y_a[:, :]).then_inc(y_a_hi, 1)
                after(u.plus(5))
                if j.first:
                    act.wait_ge(s_step, j.times(3))
                nc.scalar.activation(u_act[:, :], ps[:, 5, :],
                                     ACT.Gelu_apprx_tanh).then_inc(u_ready, 1)
                split_hi(u.plus(5 + RING))
                act.wait_ge(s_step, j.times(3, 3))
                copy_hi(c_hi[:, tile, :], y_s[:, :]).then_inc(y_s_hi, 1)

            for b in range(2):
                mix_tile(Count(U_MIX + PER_TILE * b), Count(b), b)
            with act.Fori(0, KT // 2 - 1) as i:
                for b in range(2):
                    mix_tile(Count(U_MIX + PER_TILE * (2 + b), i, 2 * PER_TILE), Count(2 + b, i, 2), b)

            def gate(u, n, b):
                after(u)
                if n.first >= 2:
                    act.wait_ge(gated, n.times(1, -1))
                nc.scalar.activation(duo[:, b, :], ps[:, 2 * b, :], ACT.Tanh,
                                     scale=0.5).then_inc(gate_ready, 1)
                split_hi(u.plus(RING))

            def behind_branch(u):
                after(u.plus(1))
                split_hi(u.plus(1 + RING))

            for b in range(2):
                gate(Count(U_GATE + 2 * b), Count(b), b)
                behind_branch(Count(U_GATE + 2 * b))
            with act.Fori(0, KT // 2 - 1) as i:
                for b in range(2):
                    u = Count(U_GATE + 4 + 2 * b, i, 4)
                    gate(u, Count(2 + b, i, 2), b)
                    behind_branch(u)
            for j in range(KT):
                u = Count(U_GATE + 2 * KT + 2 * j)
                gate(u, Count(KT + j), j % 2)
                if j in (2, 3):
                    for t in range(4 * (j - 2), 4 * (j - 1)):
                        act.wait_ge(centred, t + 1)
                        nc.scalar.activation(nrm[:, t, :], conf[:, t, :], ACT.Square).then_inc(squared, 1)
                if j == 5:
                    act.wait_ge(var_step, 2)
                    nc.scalar.activation(y_s[:, :], y_s[:, :], ACT.Sqrt).then_inc(conf_rstd, 1)
                behind_branch(u)
                for t in SILU_TILES.get(j, ()):
                    act.wait_ge(scaled, t + 1)
                    nc.scalar.activation(nrm[:, t, :], conf[:, t, :], ACT.Identity,
                                         bias=cols[:, t, COL_LN_B:COL_LN_B + 1],
                                         scale=cols[:, t, COL_LN_G:COL_LN_G + 1]).then_inc(affine, 1)
                    act.wait_ge(affine, t + 1)
                    nc.scalar.activation(conf[:, t, :], nrm[:, t, :], ACT.Tanh,
                                         scale=0.5).then_inc(silu_th, 1)
                for t in SILU_TILES.get(j, ()):
                    act.wait_ge(silu, t + 1)
                    copy_hi(b_hi[:, t, :], nrm[:, t, :], 0.5).then_inc(y_c_hi, 1)
            act.wait_ge(y_c_lo, KT)
            act.dma_start(resid[:, :, :], x_d.rearrange("(c p) n -> p c n", p=P)).then_inc(x_again, 16)
            for n, r in enumerate((ROW_MIX_POST, ROW_FFN_PRE, ROW_FFN_POST)):
                act.dma_start(row[n], rows_d[r:r + 1, :].to_broadcast([P, D])).then_inc(rows_again, 16)
            with act.Fori(0, KT // 2) as i:
                for b in range(2):
                    u = Count(U_GATE + 4 * KT + 2 * b, i, 4)
                    j = Count(b, i, 2)
                    gate(u, Count(2 * KT + b, i, 2), b)
                    after(u.plus(1))
                    act.wait_ge(merged_ready, j.times(1, KT + 1))
                    copy_hi(c_hi[:, j.times(1), :], merged[:, j.times(1), :], 0.5).then_inc(merged_hi, 1)
                    split_hi(u.plus(1 + RING))
            for n in range(CH):
                split_hi(Count(U_OUT + CH + n), resident(a_hi, n), free=False)

            def first_ff(units):
                for n in units:
                    act.wait_ge(unit_done, U_OUT + n + 1)
                    split_hi(Count(U_FF + n), free=False)

            for c in range(CH):
                if c == CH - 1:
                    turned_hi(CH + c - 1, c - 1, b_hi, 2 * (c - 1))
                for half in range(2):
                    block_whole(act, c, half, 0, U_OUT)
                    sum_squares(CH + 3 * c + half, ps[:, 2 * c + half, :],
                                by_token[:, c, half * HALF:(half + 1) * HALF])
                if 0 < c < CH - 1:
                    turned_hi(CH + c - 1, c - 1, b_hi, 2 * (c - 1))
                if c == CH - 1:
                    first_ff((2, 3))
                act.wait_ge(mixed_in, 4 * c + 3)
                sum_squares(CH + 3 * c + 2, resid[:, c, :].rearrange("p (b n) -> p b n", b=2),
                            ps[:, 2 * c:2 * c + 2, :])
                if c == CH - 2:
                    first_ff((0, 1))
            turned_hi(2 * CH - 1, CH - 1, b_hi, 2 * (CH - 1))

            def hidden_unit(u, n):
                after(u)
                if n.first % KT >= 2:
                    act.wait_ge(hidden_lo, n.times(1, -1))
                h = duo[:, n.first % 2, :]
                nc.scalar.activation(h, ps[:, n.first % KT, :], ACT.Relu).then_inc(hidden_relu, 1)
                act.wait_ge(hidden_relu, n.times(1, 1))
                nc.scalar.activation(a_hi[:, n.first % KT, :], h, ACT.Square).then_inc(hidden_hi, 1)
                split_hi(u.plus(RING))

            with act.Fori(0, QUARTERS - 1) as q:
                for n in range(KT):
                    hidden_unit(Count(U_FF + n, q, PER_QUARTER), Count(n, q, KT))
                for n in range(KT):
                    u = Count(U_FF + KT + n, q, PER_QUARTER)
                    after(u)
                    split_hi(u.plus(RING))
            for n in range(KT):
                hidden_unit(Count(U_FF + (QUARTERS - 1) * PER_QUARTER + n), Count((QUARTERS - 1) * KT + n))
            for n in range(CH):
                split_hi(Count(UNITS - CH + n), resident(c_hi, n), free=False)
            for c in range(CH):
                for half in range(2):
                    act.wait_ge(mlp_sum, ((QUARTERS - 1) * CH + c) * 2 + half + 1)
                    sum_squares(4 * CH + 2 * c + half, by_token[:, c, half * HALF:(half + 1) * HALF],
                                ps[:, 2 * c + half, :])

        @block.vector
        def _(dve):
            def lo(dst, src, hi, scale=None):
                if scale is None:
                    return nc.vector.tensor_tensor(dst, src, hi, ALU.subtract)
                return nc.vector.scalar_tensor_tensor(out=dst, in0=src, scalar=scale, in1=hi,
                                                      op0=ALU.mult, op1=ALU.subtract)

            def split_lo(u, into=None, hi=None):
                dve.wait_ge(w_hi_ready, u.times(1, 1))
                lo(w_lo[:, u.ring, :] if into is None else into, raw[:, u.raw, :],
                   w_hi[:, u.ring, :] if hi is None else hi).then_inc(w_lo_ready, 1)

            def after(u):
                dve.wait_ge(unit_done, u.times(1, 1))

            def turned_lo(n, c, hi, dst, banks):
                for g in range(2):
                    dve.wait_ge(act_hi_ready, 2 * n + g + 1)
                    lo(dst[:, 4 * g:4 * g + 4, c * P:(c + 1) * P],
                       ps[:, banks + g, :].rearrange("p (k t) -> p k t", k=4),
                       hi[:, 4 * g:4 * g + 4, c * P:(c + 1) * P]).then_inc(act_lo_ready, 1)

            dve.wait_ge(rows_loaded, 16)
            for c in range(CH):
                dve.wait_ge(x_loaded[c], 16)
                dve.wait_ge(rstd_ready, c + 1)
                nc.vector.scalar_tensor_tensor(out=by_token[:, c, :], in0=resid[:, c, :],
                                               scalar=rstd[:, c:c + 1], in1=row[0], op0=ALU.mult,
                                               op1=ALU.mult).then_inc(normed, 1)
                if c >= 2:
                    turned_lo(c - 1, c - 1, a_hi, a_lo, 2 * (c - 1))
                split_lo(Count(c))
                if c == 0:
                    turned_lo(0, 0, a_hi, a_lo, 0)
            turned_lo(CH - 1, CH - 1, a_hi, a_lo, 2 * (CH - 1))
            dve.wait_ge(cols_loaded, 16)
            taps = cols[:, :, COL_CONF:COL_CONF + CONF_K]
            nc.vector.tensor_scalar(taps, taps, 0.5, None, ALU.mult).then_inc(cols_scaled, 1)

            def statistics(half):
                for c in range(CH):
                    dve.wait_ge(v_ready, half * CH + c + 1)
                    nc.vector.bn_stats(bn[:, c, half, :],
                                       by_token[:, c, half * HALF:(half + 1) * HALF]).then_inc(bn_ready, 1)

            for n in range(2 * CH):
                u = Count(U_V + n)
                after(u)
                split_lo(u.plus(RING))
                if n == CH:
                    statistics(0)
            statistics(1)
            dve.wait_ge(bn_ready, 2 * CH)
            for c in range(CH):
                nc.vector.bn_aggr(mv[:, c, :], bn[:, c, :, :]).then_inc(bn_ready, 1)
            dve.wait_ge(v_rstd_ready, 2)
            for c in range(CH):
                nc.vector.tensor_scalar(by_token[:, c, :], by_token[:, c, :], mv[:, c, 0:1],
                                        v_rstd[:, 1, c:c + 1], ALU.subtract, ALU.mult).then_inc(v_normed, 1)
            nc.vector.memset(glu[:, :, 0:PAD], 0.0).then_inc(pads_ready, 1)
            nc.vector.memset(prod[:, 0:CONV_A - 1], 0.0).then_inc(pads_ready, 1)
            dve.wait_ge(pads_ready, 2)

            def conf_taps(tile, first, many, before):
                for n in range(many):
                    k = first + n
                    if not (isinstance(before(n), int) and before(n) == 0):
                        dve.wait_ge(conf_tap, before(n))
                    nc.vector.scalar_tensor_tensor(
                        out=conf[:, tile, :], in0=glu[:, tile, k:k + SEQ],
                        scalar=cols[:, tile, COL_CONF + k:COL_CONF + k + 1], in1=conf[:, tile, :],
                        op0=ALU.mult, op1=ALU.add).then_inc(conf_tap, 1)

            def mix_tile(u, j, b, first):
                tile = j.times(1)
                own = 0
                late = 0

                def taps_own(step):
                    nonlocal own
                    done = own
                    own += TAPS_OWN[step]
                    conf_taps(tile, 1 + done, TAPS_OWN[step],
                              lambda n: j.times(N_OWN + N_NEXT, done + n))

                def taps_next(step):
                    nonlocal late
                    if first:
                        return
                    done = late
                    late += TAPS_NEXT[step]
                    conf_taps(j.times(1, -1), 1 + N_OWN + done, TAPS_NEXT[step],
                              lambda n: j.times(N_OWN + N_NEXT, done + n - N_NEXT))

                after(u)
                split_lo(u.plus(RING))
                taps_next(0)
                after(u.plus(1))
                dve.wait_ge(th_ready, j.times(1, 1))
                nc.vector.scalar_tensor_tensor(out=glu[:, tile, PAD:], in0=th, scalar=1.0,
                                               in1=ps[:, 1, :], op0=ALU.add,
                                               op1=ALU.mult).then_inc(glu_ready, 1)
                split_lo(u.plus(1 + RING))
                taps_next(1)
                after(u.plus(2))
                split_lo(u.plus(2 + RING))
                dve.wait_ge(tap0_ready, j.times(1, 1))
                taps_own(0)
                dve.wait_ge(v_hi_ready, j.times(1, 1))
                lo(v_lo[:, :, :], by_token[:, :, bass.ds(j.times(P), P)], v_hi[:, :, :]).then_inc(v_lo_ready, 1)
                dve.wait_ge(ws_hi_ready, j.times(1, 1))
                lo(ws_lo[:, :], ws_raw[:, b, :], ws_hi[:, :]).then_inc(ws_lo_ready, 1)
                after(u.plus(3))
                dve.wait_ge(h_copied, j.times(1, 1))
                nc.vector.tensor_tensor(prod[:, CONV_A - 1:], ps[:, 3, :], h_copy,
                                        ALU.mult).then_inc(prod_ready, 1)
                split_lo(u.plus(3 + RING))
                taps_own(1)
                dve.wait_ge(a_tap0, j.times(1, 1))
                for k in range(1, CONV_A):
                    if k > 1:
                        dve.wait_ge(a_step, j.times(3, k - 1))
                    nc.vector.scalar_tensor_tensor(
                        out=y_a[:, :], in0=prod[:, k:k + SEQ],
                        scalar=cols[:, tile, COL_A + k:COL_A + k + 1], in1=y_a[:, :],
                        op0=ALU.mult, op1=ALU.add).then_inc(a_step, 1)
                after(u.plus(4))
                dve.wait_ge(a_step, j.times(3, 2))
                nc.vector.tensor_tensor(y_a[:, :], ps[:, 4, :], y_a[:, :], ALU.mult).then_inc(a_step, 1)
                split_lo(u.plus(4 + RING))
                taps_own(2)
                dve.wait_ge(y_a_hi, j.times(1, 1))
                lo(b_lo[:, tile, :], y_a[:, :], b_hi[:, tile, :]).then_inc(y_a_lo, 1)
                after(u.plus(5))
                split_lo(u.plus(5 + RING))
                dve.wait_ge(spatial_done, j.times(1, 1))
                nc.vector.scalar_tensor_tensor(out=bias[:, :], in0=ps[:, 7, 0:P],
                                               scalar=cols[:, tile, COL_SGU_B:COL_SGU_B + 1],
                                               in1=bs_row[:, b, :], op0=ALU.mult,
                                               op1=ALU.add).then_inc(s_step, 1)
                dve.wait_ge(s_step, j.times(3, 1))
                by_chunk = "p (c t) -> p c t"
                nc.vector.scalar_tensor_tensor(out=y_s[:, :].rearrange(by_chunk, c=CH),
                                               in0=ps[:, 6, :].rearrange(by_chunk, c=CH),
                                               scalar=cols[:, tile, COL_SGU_G:COL_SGU_G + 1],
                                               in1=bias[:, :].unsqueeze(1).to_broadcast([P, CH, P]),
                                               op0=ALU.mult, op1=ALU.add).then_inc(s_step, 1)
                dve.wait_ge(u_ready, j.times(1, 1))
                dve.wait_ge(s_step, j.times(3, 2))
                nc.vector.tensor_tensor(y_s[:, :], y_s[:, :], u_act[:, :], ALU.mult).then_inc(s_step, 1)
                taps_own(3)
                dve.wait_ge(y_s_hi, j.times(1, 1))
                lo(c_lo[:, tile, :], y_s[:, :], c_hi[:, tile, :]).then_inc(y_s_lo, 1)

            for b in range(2):
                mix_tile(Count(U_MIX + PER_TILE * b), Count(b), b, first=b == 0)
            with dve.Fori(0, KT // 2 - 1) as i:
                for b in range(2):
                    mix_tile(Count(U_MIX + PER_TILE * (2 + b), i, 2 * PER_TILE), Count(2 + b, i, 2), b,
                             first=False)
            last = KT - 1
            conf_taps(last, 1 + N_OWN, N_NEXT, lambda n: KT * N_OWN + last * N_NEXT + n)

            def add_branch(u, n, j, b, first=False):
                after(u.plus(1))
                dve.wait_ge(gate_ready, n.times(1, 1))
                into = merged[:, j.times(1), :] if first else y_a[:, :]
                if not first and n.first > KT:
                    dve.wait_ge(merged_ready, n.times(1, -KT))
                nc.vector.scalar_tensor_tensor(out=into, in0=duo[:, b, :], scalar=1.0,
                                               in1=ps[:, 2 * b + 1, :], op0=ALU.add,
                                               op1=ALU.mult).then_inc(gated, 1)
                if not first:
                    dve.wait_ge(gated, n.times(1, 1))
                    nc.vector.tensor_tensor(merged[:, j.times(1), :], merged[:, j.times(1), :],
                                            y_a[:, :], ALU.add).then_inc(merged_ready, 1)

            with dve.Fori(0, KT // 2) as i:
                for b in range(2):
                    u = Count(U_GATE + 2 * b, i, 4)
                    j = Count(b, i, 2)
                    after(u)
                    split_lo(u.plus(RING))
                    here = N_LATE // 2
                    base = KT * (N_OWN + N_NEXT)
                    conf_taps(j.times(1), 1 + N_OWN + N_NEXT, here,
                              lambda n: j.times(N_LATE, base + n))
                    add_branch(u, j, j, b, first=True)
                    split_lo(u.plus(1 + RING))
                    conf_taps(j.times(1), 1 + N_OWN + N_NEXT + here, N_LATE - here,
                              lambda n: j.times(N_LATE, base + here + n))
            for j in range(KT):
                u = Count(U_GATE + 2 * KT + 2 * j)
                after(u)
                split_lo(u.plus(RING))
                if j in (2, 3):
                    for t in range(4 * (j - 2), 4 * (j - 1)):
                        dve.wait_ge(stat_done, 1)
                        nc.vector.tensor_tensor(conf[:, t, :], conf[:, t, :], ps[:, 4, :],
                                                ALU.subtract).then_inc(centred, 1)
                if j == 5:
                    dve.wait_ge(stat_done, 2)
                    nc.vector.tensor_scalar(y_s[:, :], ps[:, 5, :], EPS, None, ALU.add).then_inc(var_step, 1)
                    dve.wait_ge(var_step, 1)
                    nc.vector.reciprocal(y_s[:, :], y_s[:, :]).then_inc(var_step, 1)
                for t in SILU_TILES.get(j, ()):
                    dve.wait_ge(conf_rstd, 1)
                    nc.vector.tensor_tensor(conf[:, t, :], conf[:, t, :], y_s[:, :],
                                            ALU.mult).then_inc(scaled, 1)
                add_branch(u, Count(KT + j), Count(j), j % 2)
                split_lo(u.plus(1 + RING))
                for t in SILU_TILES.get(j, ()):
                    dve.wait_ge(silu_th, t + 1)
                    nc.vector.scalar_tensor_tensor(out=nrm[:, t, :], in0=conf[:, t, :], scalar=1.0,
                                                   in1=nrm[:, t, :], op0=ALU.add,
                                                   op1=ALU.mult).then_inc(silu, 1)
                for t in SILU_TILES.get(j, ()):
                    dve.wait_ge(y_c_hi, t + 1)
                    lo(b_lo[:, t, :], nrm[:, t, :], b_hi[:, t, :], 0.5).then_inc(y_c_lo, 1)
            with dve.Fori(0, KT // 2) as i:
                for b in range(2):
                    u = Count(U_GATE + 4 * KT + 2 * b, i, 4)
                    j = Count(b, i, 2)
                    after(u)
                    split_lo(u.plus(RING))
                    add_branch(u, Count(2 * KT + b, i, 2), j, b)
                    split_lo(u.plus(1 + RING))
                    dve.wait_ge(merged_hi, j.times(1, 1))
                    lo(c_lo[:, j.times(1), :], merged[:, j.times(1), :], c_hi[:, j.times(1), :],
                       0.5).then_inc(merged_lo, 1)
            for n in range(CH):
                split_lo(Count(U_OUT + CH + n), resident(a_lo, n), resident(a_hi, n))

            dve.wait_ge(x_again, 16)
            dve.wait_ge(rows_again, 48)
            for c in range(CH):
                if c == CH - 1:
                    turned_lo(CH + c - 1, c - 1, b_hi, b_lo, 2 * (c - 1))
                for half in range(2):
                    w = slice(half * HALF, (half + 1) * HALF)
                    dve.wait_ge(meansq_ready, CH + 3 * c + half + 1)
                    nc.vector.tensor_tensor(by_token[:, c, w], ps[:, 2 * c + half, :], row[0][:, w],
                                            ALU.mult).then_inc(mixed_in, 1)
                dve.wait_ge(rstd_ready, CH + 2 * c + 1)
                dve.wait_ge(mixed_in, 4 * c + 2)
                nc.vector.scalar_tensor_tensor(out=resid[:, c, :], in0=by_token[:, c, :],
                                               scalar=rstd[:, CH + 2 * c:CH + 2 * c + 1],
                                               in1=resid[:, c, :], op0=ALU.mult,
                                               op1=ALU.add).then_inc(mixed_in, 1)
                dve.wait_ge(mixed_in, 4 * c + 3)
                nc.vector.tensor_tensor(by_token[:, c, :], resid[:, c, :], row[1],
                                        ALU.mult).then_inc(mixed_in, 1)
                if 0 < c < CH - 1:
                    turned_lo(CH + c - 1, c - 1, b_hi, b_lo, 2 * (c - 1))
                if c == CH - 1:
                    split_lo(Count(U_FF + 2))
                dve.wait_ge(rstd_ready, CH + 2 * c + 2)
                dve.wait_ge(mixed_in, 4 * c + 4)
                nc.vector.tensor_scalar(by_token[:, c, :], by_token[:, c, :],
                                        rstd[:, CH + 2 * c + 1:CH + 2 * c + 2], None,
                                        ALU.mult).then_inc(normed, 1)
                for n in {CH - 2: (0, 1), CH - 1: (3,)}.get(c, ()):
                    split_lo(Count(U_FF + n))
            turned_lo(2 * CH - 1, CH - 1, b_hi, b_lo, 2 * (CH - 1))

            def hidden_unit(u, n):
                place = n.first % KT
                h = duo[:, n.first % 2, :]
                after(u)
                split_lo(u.plus(RING))
                dve.wait_ge(hidden_hi, n.times(1, 1))
                nc.vector.tensor_tensor(h, h, h, ALU.mult).then_inc(hidden_sq, 1)
                dve.wait_ge(hidden_sq, n.times(1, 1))
                lo(a_lo[:, place, :], h, a_hi[:, place, :]).then_inc(hidden_lo, 1)

            dve.wait_ge(wide_cleared, 1)
            with dve.Fori(0, QUARTERS - 1) as q:
                for n in range(KT):
                    hidden_unit(Count(U_FF + n, q, PER_QUARTER), Count(n, q, KT))
                for n in range(KT):
                    u = Count(U_FF + KT + n, q, PER_QUARTER)
                    after(u)
                    if n % CH == CH - 1:
                        half = n // CH
                        for c in range(CH):
                            y = by_token[:, c, half * HALF:(half + 1) * HALF]
                            nc.vector.tensor_tensor(y, y, ps[:, half * CH + c, :],
                                                    ALU.add).then_inc(mlp_sum, 1)
                    split_lo(u.plus(RING))
            for n in range(KT):
                hidden_unit(Count(U_FF + (QUARTERS - 1) * PER_QUARTER + n), Count((QUARTERS - 1) * KT + n))
            for n in range(CH):
                split_lo(Count(UNITS - CH + n), resident(c_lo, n), resident(c_hi, n))

            sums = (QUARTERS - 1) * 2 * CH
            dve.wait_ge(mlp_sum, sums)
            for c in range(CH):
                for half in range(2):
                    w = slice(half * HALF, (half + 1) * HALF)
                    block_whole(dve, c, half, len(BLOCKS) - 2, UNITS - KT)
                    nc.vector.tensor_tensor(by_token[:, c, w], by_token[:, c, w],
                                            ps[:, 2 * c + half, :], ALU.add).then_inc(mlp_sum, 1)
                    if c:
                        dve.wait_ge(out_ready, 2 * c)
                    dve.wait_ge(mlp_sum, sums + 2 * c + half + 1)
                    nc.vector.tensor_tensor(weighted[:, w], by_token[:, c, w], row[2][:, w],
                                            ALU.mult).then_inc(out_weighted, 1)
                dve.wait_ge(rstd_ready, 3 * CH + c + 1)
                for half in range(2):
                    w = slice(half * HALF, (half + 1) * HALF)
                    dve.wait_ge(out_weighted, 2 * c + half + 1)
                    nc.vector.scalar_tensor_tensor(out=by_token[:, c, w], in0=weighted[:, w],
                                                   scalar=rstd[:, 3 * CH + c:3 * CH + c + 1],
                                                   in1=resid[:, c, w], op0=ALU.mult,
                                                   op1=ALU.add).then_inc(out_ready, 1)

        @block.tensor
        def _(pe):
            def products(bank, left_hi, left_lo, right_hi, right_lo, first, final):
                nc.tensor.matmul(ps[:, bank, :], left_hi, right_hi, start=first, stop=False)
                nc.tensor.matmul(ps[:, bank, :], left_hi, right_lo, start=False, stop=False)
                return nc.tensor.matmul(ps[:, bank, :], left_lo, right_hi, start=False, stop=final)

            def ready(u):
                pe.wait_ge(w_lo_ready, u.times(1, 1))

            def channel_unit(u, hi, low, bank, before_tile=None):
                ready(u)
                for k in range(KT):
                    if before_tile:
                        before_tile(k)
                    w = slice(k * P, (k + 1) * P)
                    mm = products(bank, w_hi[:, u.ring, w], w_lo[:, u.ring, w], hi[:, k, :], low[:, k, :],
                                  k == 0, k == KT - 1)
                mm.then_inc(unit_done, 1)

            def token_block(c, piece, hi, low, right_hi, right_lo, bank):
                for n in range(2):
                    k = 2 * piece + n
                    t, w = slice(c * P, (c + 1) * P), slice(n * HALF, (n + 1) * HALF)
                    mm = products(bank, hi[:, k, t], low[:, k, t], right_hi[:, w], right_lo[:, w],
                                  k == 0, k == KT - 1)
                return mm

            def token_unit(u, piece, half, hi, low):
                ready(u)
                for c in range(CH):
                    mm = token_block(c, piece, hi, low, w_hi[:, u.ring, :], w_lo[:, u.ring, :],
                                     half * CH + c)
                mm.then_inc(unit_done, 1)

            def turn(n, c, banks):
                pe.wait_ge(normed, n + 1)
                for g in range(2):
                    for k in range(4):
                        at = (4 * g + k) * P
                        mm = nc.tensor.transpose(ps[:, banks + g, k * P:(k + 1) * P],
                                                 by_token[:, c, at:at + P], ident[:, :])
                    mm.then_inc(turned, 1)

            def resident_products(first_unit, hi, low, second_hi, second_lo, before_piece, between):
                for n, piece in BLOCK_PIECES:
                    c, half = BLOCKS[n]
                    u = Count(first_unit + half * CH + piece)
                    if c == 0:
                        ready(u)
                        if half == 0:
                            before_piece(piece)
                    w = ((w_hi[:, u.ring, :], w_lo[:, u.ring, :]) if half == 0 else
                         (resident(second_hi, piece), resident(second_lo, piece)))
                    mm = token_block(c, piece, hi, low, *w, 2 * c + half)
                    if c == CH - 1:
                        mm.then_inc(unit_done, 1)
                    elif piece == CH - 1:
                        mm.then_inc(block_done, 1)
                    between(n, piece)

            def s_v_block(c, n):
                u = Count(U_V + n)
                return token_block(c, n, a_hi, a_lo, w_hi[:, u.ring, :], w_lo[:, u.ring, :], c)

            pe.wait_ge(consts_ready, 5)
            turn(0, 0, 0)

            for n in range(CH):
                pe.wait_ge(act_lo_ready, 2 * (n + 1))
                for older in range(n):
                    mm = s_v_block(n, older)
                    if n == CH - 1:
                        mm.then_inc(unit_done, 1)
                ready(Count(U_V + n))
                for c in range(n + 1):
                    mm = s_v_block(c, n)
                for c in {0: (1, 2), 1: (3,)}.get(n, ()):
                    turn(c, c, 2 * c)
            mm.then_inc(unit_done, 1)
            for n in range(CH, 2 * CH):
                token_unit(Count(U_V + n), n % CH, n // CH, a_hi, a_lo)

            with pe.Fori(0, KT // 2) as i:
                for b in range(2):
                    j = Count(b, i, 2)
                    for n in range(PER_TILE):
                        channel_unit(Count(U_MIX + PER_TILE * b + n, i, 2 * PER_TILE), a_hi, a_lo, n)
                    pe.wait_ge(v_lo_ready, j.times(1, 1))
                    pe.wait_ge(ws_lo_ready, j.times(1, 1))
                    out = ps[:, 7, 0:P]
                    nc.tensor.matmul(out, ones[:, :], ws_hi[:, :], start=True, stop=False)
                    nc.tensor.matmul(out, ones[:, :], ws_lo[:, :], start=False, stop=True)
                    for c in range(CH):
                        out = ps[:, 6, c * P:(c + 1) * P]
                        nc.tensor.matmul(out, v_hi[:, c, :], ws_hi[:, :], start=True, stop=False)
                        nc.tensor.matmul(out, v_hi[:, c, :], ws_lo[:, :], start=False, stop=False)
                        mm = nc.tensor.matmul(out, v_lo[:, c, :], ws_hi[:, :], start=False, stop=True)
                    mm.then_inc(spatial_done, 1)

            def pair(u, hi, low, b, whole=None):
                channel_unit(u, a_hi, a_lo, 2 * b)
                if whole is not None:
                    pe.wait_ge(whole, KT)
                channel_unit(u.plus(1), hi, low, 2 * b + 1)

            with pe.Fori(0, KT // 2) as i:
                for b in range(2):
                    pair(Count(U_GATE + 2 * b, i, 4), b_hi, b_lo, b, y_a_lo)
            for j in range(KT):
                pair(Count(U_GATE + 2 * KT + 2 * j), c_hi, c_lo, j % 2, y_s_lo)
                if j == 1:
                    pe.wait_ge(chan_sum, KT)
                    nc.tensor.matmul(ps[:, 4, :], mean_of[:, :], u_act[:, :], start=True,
                                     stop=True).then_inc(stat_done, 1)
                if j == 4:
                    pe.wait_ge(sq_sum, KT - 1)
                    nc.tensor.matmul(ps[:, 5, :], mean_of[:, :], nrm[:, 0, :], start=True,
                                     stop=True).then_inc(stat_done, 1)
            first_gate = Count(U_GATE + 4 * KT)
            channel_unit(first_gate, a_hi, a_lo, 0)
            channel_unit(first_gate.plus(1), b_hi, b_lo, 1, lambda k: pe.wait_ge(y_c_lo, k + 1))
            pair(first_gate.plus(2), b_hi, b_lo, 1)
            with pe.Fori(0, KT // 2 - 1) as i:
                for b in range(2):
                    pair(Count(U_GATE + 4 * KT + 4 + 2 * b, i, 4), b_hi, b_lo, b)

            def turn_between(n, piece):
                for c in range(CH - 1):
                    if (n, piece) == (BLOCKS.index((c, 1)) + 2, 1):
                        turn(CH + c, c, 2 * c)

            resident_products(U_OUT, c_hi, c_lo, a_hi, a_lo,
                              lambda piece: pe.wait_ge(merged_lo, 2 * piece + 2), turn_between)

            def early_unit(u, n, tokens):
                for k in range(KT):
                    w = slice(k * P, (k + 1) * P)
                    out = ps[:, n, tokens]
                    nc.tensor.matmul(out, w_hi[:, u.ring, w], b_hi[:, k, tokens], start=k == 0, stop=False)
                    nc.tensor.matmul(out, w_hi[:, u.ring, w], b_lo[:, k, tokens], start=False, stop=False)
                    mm = nc.tensor.matmul(out, w_lo[:, u.ring, w], b_hi[:, k, tokens], start=False,
                                          stop=k == KT - 1)
                return mm

            pe.wait_ge(act_lo_ready, 4 * CH - 2)
            for n in range(EARLY):
                if n == EARLY - 1:
                    turn(2 * CH - 1, CH - 1, 2 * (CH - 1))
                ready(Count(U_FF + n))
                early_unit(Count(U_FF + n), n, slice(0, (CH - 1) * P))
            pe.wait_ge(act_lo_ready, 4 * CH)
            for n in range(EARLY):
                early_unit(Count(U_FF + n), n, slice((CH - 1) * P, SEQ)).then_inc(unit_done, 1)

            def up(u, n):
                channel_unit(u, b_hi, b_lo, n)

            with pe.Fori(0, QUARTERS - 1) as q:
                for n in range(EARLY, KT):
                    up(Count(U_FF + n, q, PER_QUARTER), n)
                for n in range(KT):
                    if n < CH:
                        pe.wait_ge(hidden_lo, Count(0, q, KT).times(1, 2 * n + 2))
                    token_unit(Count(U_FF + KT + n, q, PER_QUARTER), n % CH, n // CH, a_hi, a_lo)
                for n in range(EARLY):
                    up(Count(U_FF + PER_QUARTER + n, q, PER_QUARTER), n)
            for n in range(EARLY, KT):
                up(Count(U_FF + (QUARTERS - 1) * PER_QUARTER + n), n)
            before = (QUARTERS - 1) * KT
            resident_products(UNITS - KT, a_hi, a_lo, c_hi, c_lo,
                              lambda piece: pe.wait_ge(hidden_lo, before + 2 * piece + 2),
                              lambda n, piece: None)


SILU_TILES = {5: (0,), 6: (1, 2, 3), 7: (4, 5, 6, 7)}


def resident(buffer, n):
    return buffer[:, 2 * n:2 * n + 2, :].rearrange("p k t -> p (k t)")


def kernel(x, norm_mix_pre, norm_mix_post, norm_ffn_pre, norm_ffn_post, w_in, conv_a_w, conf_dw_w,
           conf_dw_b, conf_ln_g, conf_ln_b, sgu_ln_g, sgu_ln_b, sgu_ws, sgu_b, w_branch, w_out,
           w_ff1, w_ff2):
    import numpy as np
    import concourse.bacc as bacc
    from concourse.bass_utils import run_bass_kernel_spmd

    def channel_units(w):
        return w.reshape(KT, P, -1, P).transpose(2, 1, 0, 3).reshape(-1, P, D)

    def token_units(w):
        return w.reshape(CH, 2, P, 2, HALF).transpose(3, 0, 2, 1, 4).reshape(-1, P, D)

    a_h, a_b, a_c, c_a, c_g, s_u, s_v, g_a, g_c, g_s = np.split(np.asarray(w_in)[0], 10, axis=1)
    w_branch, w_out = np.asarray(w_branch)[0], np.asarray(w_out)[0]
    w_ff1, w_ff2 = np.asarray(w_ff1)[0], np.asarray(w_ff2)[0]

    def interleave(*parts):
        return np.stack([channel_units(p) for p in parts], axis=1).reshape(-1, P, D)

    units = [token_units(s_v), interleave(c_g, c_a, a_h, a_c, a_b, s_u), interleave(g_a, w_branch[0]),
             interleave(g_s, w_branch[2]), interleave(g_c, w_branch[1]), token_units(w_out)]
    for q in range(QUARTERS):
        units += [channel_units(w_ff1[:, q * D:(q + 1) * D]), token_units(w_ff2[q * D:(q + 1) * D])]
    by_channel = np.concatenate([np.asarray(a)[0].reshape(-1, D) for a in
                                 (conv_a_w, conf_dw_w, conf_dw_b, conf_ln_g, conf_ln_b, sgu_ln_g, sgu_ln_b)])
    arrays = {
        "x_in": np.asarray(x)[0],
        "units_in": np.concatenate(units),
        "cols_in": by_channel.reshape(COLS, KT, P).transpose(2, 1, 0),
        "rows_in": np.concatenate([np.asarray(a) for a in
                                   (norm_mix_pre, norm_mix_post, norm_ffn_pre, norm_ffn_post)]),
        "ws_in": np.asarray(sgu_ws)[0].transpose(0, 2, 1),
        "bs_in": np.asarray(sgu_b)[0],
    }
    arrays = {name: np.ascontiguousarray(a) for name, a in arrays.items()}
    nc = bacc.Bacc("TRN2", target_bir_lowering=False, num_devices=1)
    ins = [nc.dram_tensor(name, a.shape, F32, kind="ExternalInput").ap() for name, a in arrays.items()]
    out = nc.dram_tensor("y_out", (SEQ, D), F32, kind="ExternalOutput").ap()
    build(nc, *ins, out)
    result = run_bass_kernel_spmd(nc, [arrays], core_ids=[0])
    return result.results[0]["y_out"].reshape(1, SEQ, D)
```
